# Optimizing a Trainium2 kernel written in Bass

```python
import jax
import jax.numpy as jnp
from jax import lax
import numpy as np
import jax, jax.numpy as jnp

D_MODEL = 1024
BATCH = 1
SEQ = 256
DEPTH = 2

HEAD_DIM = 64
ROT_DIM = HEAD_DIM // 4
ROPE_THETA = 500000.0
DIL_GROUPS = ((128, 1), (512, 4), (2048, 16))
HEADS_PER_DIL_GROUP = 2
N_HEADS_A = len(DIL_GROUPS) * HEADS_PER_DIL_GROUP
N_HEADS_B = 6
N_HEADS_M = 4
MOBA_BLOCK = 256
MOBA_TOPK = 3
MOBA_Q_CHUNK = 32
N_MEM = 256
D_FF = 4 * D_MODEL
N_BRANCH = 3
WIDTH_A = N_HEADS_A * HEAD_DIM
WIDTH_A_OUT = HEADS_PER_DIL_GROUP * HEAD_DIM
WIDTH_B = N_HEADS_B * HEAD_DIM
WIDTH_M = N_HEADS_M * HEAD_DIM
D_IN = 3 * WIDTH_A + 3 * WIDTH_B + WIDTH_M + N_BRANCH * D_MODEL
RMS_EPS = 1e-6
NEG_INF = -1e30


def rms_norm(x, g):
    xf = x.astype(jnp.float32)
    y = xf * lax.rsqrt(jnp.mean(xf * xf, axis=-1, keepdims=True) + RMS_EPS)
    return (y * g.astype(jnp.float32)).astype(x.dtype)

def partial_rope(x, pos):
    inv_freq = 1.0 / (ROPE_THETA ** (jnp.arange(0, ROT_DIM, 2, dtype=jnp.float32) / ROT_DIM))
    ang = pos.astype(jnp.float32)[:, None] * inv_freq[None, :]
    cos = jnp.cos(ang)[None, :, None, :]
    sin = jnp.sin(ang)[None, :, None, :]
    xr = x[..., :ROT_DIM].astype(jnp.float32)
    x1, x2 = xr[..., :ROT_DIM // 2], xr[..., ROT_DIM // 2:]
    rot = jnp.concatenate([x1 * cos - x2 * sin, x2 * cos + x1 * sin], axis=-1).astype(x.dtype)
    return jnp.concatenate([rot, x[..., ROT_DIM:]], axis=-1)

def dilated_window_attn(q, k, v, window, dilation):
    B, S, H, Dh = q.shape
    n = window // dilation
    span = n * dilation
    Sp = -(-S // span) * span
    L = Sp // dilation
    nblk = L // n

    def to_blocks(t):
        t = jnp.pad(t, ((0, 0), (0, Sp - S), (0, 0), (0, 0)))
        t = t.reshape(B, L, dilation, H, Dh).transpose(0, 2, 3, 1, 4)
        return t.reshape(B, dilation, H, nblk, n, Dh)

    def with_prev(t):
        prev = jnp.pad(t, ((0, 0), (0, 0), (0, 0), (1, 0), (0, 0), (0, 0)))[:, :, :, :-1]
        return jnp.concatenate([prev, t], axis=-2)

    qb = to_blocks(q)
    kk = with_prev(to_blocks(k))
    vv = with_prev(to_blocks(v))
    s = jnp.einsum('brhnqd,brhnkd->brhnqk', qb, kk).astype(jnp.float32)
    i = jnp.arange(n)[:, None]
    j = jnp.arange(2 * n)[None, :]
    band = (j >= i) & (j <= i + n)
    first = (jnp.arange(nblk) == 0)[:, None, None] & (j < n)[None]
    mask = band[None] & ~first
    s = jnp.where(mask, s, NEG_INF)
    mx = jnp.max(s, axis=-1, keepdims=True)
    p = jnp.exp(s - mx)
    den = jnp.sum(p, axis=-1, keepdims=True)
    o = jnp.einsum('brhnqk,brhnkd->brhnqd', (p / den).astype(v.dtype), vv)
    lse = (mx + jnp.log(den))[..., 0]
    o = o.reshape(B, dilation, H, L, Dh).transpose(0, 3, 1, 2, 4).reshape(B, Sp, H, Dh)[:, :S]
    lse = lse.reshape(B, dilation, H, L).transpose(0, 3, 1, 2).reshape(B, Sp, H)[:, :S]
    return o, lse

def dilated_mixer(q, k, v):
    B, S = q.shape[0], q.shape[1]
    outs, lses = [], []
    for g, (win, dil) in enumerate(DIL_GROUPS):
        sl = slice(g * HEADS_PER_DIL_GROUP, (g + 1) * HEADS_PER_DIL_GROUP)
        o, l = dilated_window_attn(q[:, :, sl], k[:, :, sl], v[:, :, sl], win, dil)
        outs.append(o)
        lses.append(l)
    w = jax.nn.softmax(jnp.stack(lses, axis=0), axis=0)
    o = jnp.einsum('gbsh,gbshd->bshd', w, jnp.stack(outs, axis=0).astype(jnp.float32))
    return o.astype(q.dtype).reshape(B, S, WIDTH_A_OUT)

def moba_attn(q, k, v):
    B, S, H, Dh = q.shape
    nB = -(-S // MOBA_BLOCK)
    Sp = nB * MOBA_BLOCK
    padw = ((0, 0), (0, Sp - S), (0, 0), (0, 0))
    qt = jnp.pad(q, padw).transpose(0, 2, 1, 3)
    kt = jnp.pad(k, padw).transpose(0, 2, 1, 3)
    vt = jnp.pad(v, padw).transpose(0, 2, 1, 3)
    kb = kt.reshape(B, H, nB, MOBA_BLOCK, Dh)
    vb = vt.reshape(B, H, nB, MOBA_BLOCK, Dh)
    qpos = jnp.arange(Sp, dtype=jnp.int32)
    qblk = qpos // MOBA_BLOCK
    own = jnp.broadcast_to(qblk[None, None, :, None], (B, H, Sp, 1))
    n_sel = min(MOBA_TOPK, nB - 1)
    if n_sel > 0:
        kmean = jnp.mean(kb.astype(jnp.float32), axis=3)
        gate = jnp.einsum('bhsd,bhnd->bhsn', qt.astype(jnp.float32), kmean)
        past = jnp.arange(nB, dtype=jnp.int32)[None, :] < qblk[:, None]
        _, top_idx = lax.top_k(jnp.where(past, gate, NEG_INF), n_sel)
        top_ok = jnp.take_along_axis(jnp.broadcast_to(past, gate.shape), top_idx, axis=-1)
        blk_idx = jnp.concatenate([top_idx.astype(jnp.int32), own], axis=-1)
        blk_ok = jnp.concatenate([top_ok, jnp.ones_like(own, dtype=bool)], axis=-1)
    else:
        blk_idx = own
        blk_ok = jnp.ones_like(own, dtype=bool)
    n_tot = blk_idx.shape[-1]
    nc = Sp // MOBA_Q_CHUNK
    C = MOBA_Q_CHUNK
    q_c = qt.reshape(B, H, nc, C, Dh).transpose(2, 0, 1, 3, 4)
    idx_c = blk_idx.reshape(B, H, nc, C, n_tot).transpose(2, 0, 1, 3, 4)
    ok_c = blk_ok.reshape(B, H, nc, C, n_tot).transpose(2, 0, 1, 3, 4)
    pos_c = qpos.reshape(nc, C)
    bi = jnp.arange(B)[:, None, None, None]
    hi = jnp.arange(H)[None, :, None, None]
    offs = jnp.arange(MOBA_BLOCK, dtype=jnp.int32)

    def chunk(args):
        qc, ic, okc, pc = args
        ks = kb[bi, hi, ic]
        vs = vb[bi, hi, ic]
        s = jnp.einsum('bhcd,bhcnkd->bhcnk', qc, ks).astype(jnp.float32)
        kpos = ic[..., None] * MOBA_BLOCK + offs
        mask = okc[..., None] & (kpos <= pc[None, None, :, None, None])
        s = jnp.where(mask, s, NEG_INF).reshape(B, H, C, n_tot * MOBA_BLOCK)
        p = jax.nn.softmax(s, axis=-1).reshape(B, H, C, n_tot, MOBA_BLOCK)
        return jnp.einsum('bhcnk,bhcnkd->bhcd', p.astype(vs.dtype), vs)

    o = lax.map(chunk, (q_c, idx_c, ok_c, pos_c))
    o = o.transpose(1, 2, 0, 3, 4).reshape(B, H, Sp, Dh)
    return o.transpose(0, 2, 1, 3)[:, :S]

def memory_attn(q, mem_n, w_mkv):
    B, S = q.shape[0], q.shape[1]
    M = mem_n.shape[1]
    kv = (mem_n @ w_mkv).reshape(B, M, 2, N_HEADS_M, HEAD_DIM)
    s = jnp.einsum('bshd,bmhd->bhsm', q, kv[:, :, 0]).astype(jnp.float32)
    p = jax.nn.softmax(s, axis=-1)
    o = jnp.einsum('bhsm,bmhd->bshd', p.astype(q.dtype), kv[:, :, 1])
    return o.reshape(B, S, WIDTH_M)

def hybrid_layer(x, mem, pos, g_mix, w_in, w_pa, w_pb, w_pm, w_o, g_mem, w_mkv, g_mlp, w_up, w_down):
    B, S, _ = x.shape
    scale = HEAD_DIM ** -0.5
    h = rms_norm(x, g_mix)
    z = h @ w_in
    o1 = 3 * WIDTH_A
    o2 = o1 + 3 * WIDTH_B
    o3 = o2 + WIDTH_M
    qkv_a = z[..., :o1].reshape(B, S, 3, N_HEADS_A, HEAD_DIM)
    qkv_b = z[..., o1:o2].reshape(B, S, 3, N_HEADS_B, HEAD_DIM)
    q_m = z[..., o2:o3].reshape(B, S, N_HEADS_M, HEAD_DIM)
    gates = jax.nn.sigmoid(z[..., o3:].reshape(B, S, N_BRANCH, D_MODEL))
    o_a = dilated_mixer(partial_rope(qkv_a[:, :, 0], pos) * scale,
                        partial_rope(qkv_a[:, :, 1], pos), qkv_a[:, :, 2])
    o_b = moba_attn(partial_rope(qkv_b[:, :, 0], pos) * scale,
                    partial_rope(qkv_b[:, :, 1], pos), qkv_b[:, :, 2]).reshape(B, S, WIDTH_B)
    o_m = memory_attn(q_m * scale, rms_norm(mem, g_mem), w_mkv)
    y = (gates[:, :, 0] * (o_a @ w_pa) + gates[:, :, 1] * (o_b @ w_pb)
         + gates[:, :, 2] * (o_m @ w_pm))
    x = x + y @ w_o
    hm = rms_norm(x, g_mlp)
    x = x + jnp.square(jax.nn.relu(hm @ w_up)) @ w_down
    return x

def first_inputs(seed: int = 0) -> dict:
    key = jax.random.key(seed)
    ks = jax.random.split(key, 16)

    def nrm(k, shape, fan_in):
        return jax.random.normal(k, shape, jnp.float32) * (fan_in ** -0.5)

    def gain(k, shape):
        return 1.0 + 0.05 * jax.random.normal(k, shape, jnp.float32)

    return {
        'x': jax.random.normal(ks[0], (BATCH, SEQ, D_MODEL), jnp.float32),
        'mem': jax.random.normal(ks[1], (BATCH, N_MEM, D_MODEL), jnp.float32),
        'norm_mix': gain(ks[2], (DEPTH, D_MODEL)),
        'w_in': nrm(ks[3], (DEPTH, D_MODEL, D_IN), D_MODEL),
        'w_proj_a': nrm(ks[4], (DEPTH, WIDTH_A_OUT, D_MODEL), WIDTH_A_OUT),
        'w_proj_b': nrm(ks[5], (DEPTH, WIDTH_B, D_MODEL), WIDTH_B),
        'w_proj_m': nrm(ks[6], (DEPTH, WIDTH_M, D_MODEL), WIDTH_M),
        'w_out': nrm(ks[7], (DEPTH, D_MODEL, D_MODEL), D_MODEL),
        'norm_mem': gain(ks[8], (DEPTH, D_MODEL)),
        'w_mem_kv': nrm(ks[9], (DEPTH, D_MODEL, 2 * WIDTH_M), D_MODEL),
        'norm_mlp': gain(ks[10], (DEPTH, D_MODEL)),
        'w_up': nrm(ks[11], (DEPTH, D_MODEL, D_FF), D_MODEL),
        'w_down': nrm(ks[12], (DEPTH, D_FF, D_MODEL), D_FF),
        'norm_final': gain(ks[13], (D_MODEL,)),
    }

def first_block(x, mem, norm_mix, w_in, w_proj_a, w_proj_b, w_proj_m, w_out, norm_mem, w_mem_kv,
              norm_mlp, w_up, w_down, norm_final):
    pos = jnp.arange(x.shape[1], dtype=jnp.int32)
    for l in range(DEPTH):
        x = hybrid_layer(x, mem, pos, norm_mix[l], w_in[l], w_proj_a[l], w_proj_b[l], w_proj_m[l],
                         w_out[l], norm_mem[l], w_mem_kv[l], norm_mlp[l], w_up[l], w_down[l])
    return rms_norm(x, norm_final)


DEPTH_2 = 1

GRID_W = 64
CTX_LEN = 256
MLA_HEADS = 8
QK_NOPE = 128
QK_ROPE = 64
V_DIM = 128
Q_LORA = 384
KV_LORA = 256
ROPE_BASE = 10000.0
ROPE_PAIRS = QK_ROPE // 4
Q_BLOCK = 128
ATTN_SCALE = (QK_NOPE + QK_ROPE) ** -0.5
MLA_WIDTH = MLA_HEADS * V_DIM
ML_HEADS = 4
ML_INNER = 1024
ML_HEAD_DIM = ML_INNER // ML_HEADS
QKV_BLOCK = 4
QKV_NBLK = ML_INNER // QKV_BLOCK
CONV_W = 5
CHUNK = 128
N_EXPERTS = 16
EXPERT_FF = 1024
CAP_FACTOR = 2
EPS = 1e-6
IN_SIZES = (Q_LORA, KV_LORA, QK_ROPE, ML_INNER, ML_INNER, D_MODEL, D_MODEL)
IN_DIM = Q_LORA + KV_LORA + QK_ROPE + 2 * ML_INNER + 2 * D_MODEL


def rmsnorm(x, g):
    xf = x.astype(jnp.float32)
    y = xf * lax.rsqrt(jnp.mean(xf * xf, axis=-1, keepdims=True) + EPS)
    return (y * g.astype(jnp.float32)).astype(x.dtype)

def modulate(h, shift, scale):
    return h * (1 + scale[:, None, :]) + shift[:, None, :]

def axial_angles(T):
    rows = T // GRID_W
    row = jnp.repeat(jnp.arange(rows, dtype=jnp.float32), GRID_W)
    col = jnp.tile(jnp.arange(GRID_W, dtype=jnp.float32), rows)
    inv = ROPE_BASE ** (-jnp.arange(ROPE_PAIRS, dtype=jnp.float32) / ROPE_PAIRS)
    return row[:, None] * inv, col[:, None] * inv

def rotate(x, ang):
    cos = jnp.cos(ang)[None, :, None, :]
    sin = jnp.sin(ang)[None, :, None, :]
    xf = x.astype(jnp.float32)
    x1, x2 = xf[..., :ROPE_PAIRS], xf[..., ROPE_PAIRS:]
    return jnp.concatenate([x1 * cos - x2 * sin, x2 * cos + x1 * sin], -1).astype(x.dtype)

def rope_2d(x, ang_row, ang_col):
    half = QK_ROPE // 2
    return jnp.concatenate([rotate(x[..., :half], ang_row), rotate(x[..., half:], ang_col)], -1)

def mla_qkv(q_lat, kv_lat, k_rope, q_norm, w_uq, kv_norm, w_ukv, angles):
    B, T, _ = q_lat.shape
    q = (rmsnorm(q_lat, q_norm) @ w_uq).reshape(B, T, MLA_HEADS, QK_NOPE + QK_ROPE)
    kv = (rmsnorm(kv_lat, kv_norm) @ w_ukv).reshape(B, T, MLA_HEADS, QK_NOPE + V_DIM)
    q_nope, q_pe = q[..., :QK_NOPE], q[..., QK_NOPE:]
    k_nope, v = kv[..., :QK_NOPE], kv[..., QK_NOPE:]
    k_pe = k_rope[:, :, None, :]
    if angles is not None:
        q_pe = rope_2d(q_pe, *angles)
        k_pe = rope_2d(k_pe, *angles)
    k_pe = jnp.broadcast_to(k_pe, (B, T, MLA_HEADS, QK_ROPE))
    return (jnp.concatenate([q_nope, q_pe], -1), jnp.concatenate([k_nope, k_pe], -1), v)

def attend(q, k, v):
    B, Tq, H, Dk = q.shape
    nb = Tq // Q_BLOCK
    qb = q.reshape(B, nb, Q_BLOCK, H, Dk).transpose(1, 0, 2, 3, 4)

    def one_block(qi):
        s = jnp.einsum('bqhd,bkhd->bhqk', qi, k).astype(jnp.float32) * ATTN_SCALE
        p = jax.nn.softmax(s, axis=-1).astype(v.dtype)
        return jnp.einsum('bhqk,bkhd->bqhd', p, v)

    o = lax.map(one_block, qb)
    return o.transpose(1, 0, 2, 3, 4).reshape(B, Tq, H * v.shape[-1])

def dwconv(x, w, b):
    out = lax.conv_general_dilated(x, w[:, None, :].astype(x.dtype), (1,), [(CONV_W // 2, CONV_W // 2)],
                                   dimension_numbers=('NWC', 'WIO', 'NWC'), feature_group_count=x.shape[-1])
    return out + b

def blockdiag(x, w):
    B, T, _ = x.shape
    y = jnp.einsum('btnj,njk->btnk', x.reshape(B, T, QKV_NBLK, QKV_BLOCK), w)
    return y.reshape(B, T, ML_INNER)

def mlstm_features(x_m, conv_w, conv_b, w_qblk, w_kblk, w_vblk, w_gate, b_gate):
    B, T, _ = x_m.shape
    x_c = jax.nn.silu(dwconv(x_m, conv_w, conv_b))
    q = blockdiag(x_c, w_qblk)
    k = blockdiag(x_c, w_kblk)
    v = blockdiag(x_m, w_vblk)
    gates = (jnp.concatenate([q, k, v], -1) @ w_gate + b_gate).reshape(B, T, 2, 2, ML_HEADS)
    gates = gates.astype(jnp.float32).transpose(2, 3, 0, 4, 1)
    heads = lambda a: a.reshape(B, T, ML_HEADS, ML_HEAD_DIM).transpose(0, 2, 1, 3).astype(jnp.float32)
    return heads(q), heads(k) * (ML_HEAD_DIM ** -0.5), heads(v), gates, x_c

def mlstm_chunkwise(q, k, v, ig, lf, state):
    B, H, T, dh = q.shape
    nc = T // CHUNK
    ch = lambda a: jnp.moveaxis(a.reshape(B, H, nc, CHUNK, *a.shape[3:]), 2, 0)
    mask = jnp.tril(jnp.ones((CHUNK, CHUNK), dtype=bool))

    def step(carry, xs):
        C, n, m = carry
        qc, kc, vc, ic, fc = xs
        b = jnp.cumsum(fc, axis=-1)
        dmat = jnp.where(mask, b[..., :, None] - b[..., None, :] + ic[..., None, :], -jnp.inf)
        inter = b + m[..., None]
        m_t = jnp.maximum(inter, jnp.max(dmat, axis=-1))
        w_inter = jnp.exp(inter - m_t)
        s = jnp.einsum('bhtd,bhsd->bhts', qc, kc) * jnp.exp(dmat - m_t[..., None])
        num = jnp.einsum('bhts,bhsd->bhtd', s, vc) + w_inter[..., None] * jnp.einsum('bhvd,bhtd->bhtv', C, qc)
        den = jnp.sum(s, axis=-1) + w_inter * jnp.einsum('bhd,bhtd->bht', n, qc)
        h = num / jnp.maximum(jnp.abs(den), jnp.exp(-m_t))[..., None]
        b_last = b[..., -1]
        dec = b_last[..., None] - b + ic
        m_new = jnp.maximum(b_last + m, jnp.max(dec, axis=-1))
        wk = jnp.exp(dec - m_new[..., None])
        keep = jnp.exp(b_last + m - m_new)
        C_new = keep[..., None, None] * C + jnp.einsum('bhsv,bhsd->bhvd', vc * wk[..., None], kc)
        n_new = keep[..., None] * n + jnp.einsum('bhs,bhsd->bhd', wk, kc)
        return (C_new, n_new, m_new), h

    state, hs = lax.scan(step, state, (ch(q), ch(k), ch(v), ch(ig), ch(lf)))
    return jnp.moveaxis(hs, 0, 2).reshape(B, H, T, dh), state

def mlstm_bidir(feat_c, feat_l):
    qc, kc, vc, gc = feat_c
    ql, kl, vl, gl = feat_l
    B, H, _, dh = qc.shape
    zero = (jnp.zeros((B, H, dh, dh), jnp.float32), jnp.zeros((B, H, dh), jnp.float32),
            jnp.zeros((B, H), jnp.float32))
    lsig = jax.nn.log_sigmoid
    flip = lambda a: jnp.flip(a, axis=2)
    hc_f, st_f = mlstm_chunkwise(qc, kc, vc, gc[0, 0], lsig(gc[0, 1]), zero)
    hl_f, _ = mlstm_chunkwise(ql, kl, vl, gl[0, 0], lsig(gl[0, 1]), st_f)
    hc_b, st_b = mlstm_chunkwise(flip(qc), flip(kc), flip(vc), flip(gc[1, 0]), lsig(flip(gc[1, 1])), zero)
    hl_b, _ = mlstm_chunkwise(flip(ql), flip(kl), flip(vl), flip(gl[1, 0]), lsig(flip(gl[1, 1])), st_b)
    return hc_f + flip(hc_b), hl_f + flip(hl_b)

def mlstm_readout(h, z, x_c, ml_norm, ml_skip):
    B, H, T, dh = h.shape
    hf = h.transpose(0, 2, 1, 3)
    hn = hf * lax.rsqrt(jnp.mean(hf * hf, axis=-1, keepdims=True) + EPS)
    hn = hn.reshape(B, T, ML_INNER).astype(z.dtype) * ml_norm
    return jax.nn.sigmoid(z) * (hn + ml_skip * x_c)

def merge(y_mla, y_ml, g_mla, g_ml, w_out):
    return (jax.nn.sigmoid(g_mla) * y_mla + jax.nn.sigmoid(g_ml) * y_ml) @ w_out

def mixer(h_c, h_l, angles, last, w_in, q_norm, w_uq, kv_norm, w_ukv, conv_w, conv_b,
          w_qblk, w_kblk, w_vblk, w_gate, b_gate, ml_norm, ml_skip, w_out):
    splits = [int(s) for s in np.cumsum(IN_SIZES)[:-1]]
    qlat_c, kvlat_c, krope_c, xm_c, z_c, gmla_c, gml_c = jnp.split(h_c @ w_in, splits, axis=-1)
    qlat_l, kvlat_l, krope_l, xm_l, z_l, gmla_l, gml_l = jnp.split(h_l @ w_in, splits, axis=-1)
    q_c, k_c, v_c = mla_qkv(qlat_c, kvlat_c, krope_c, q_norm, w_uq, kv_norm, w_ukv, None)
    q_l, k_l, v_l = mla_qkv(qlat_l, kvlat_l, krope_l, q_norm, w_uq, kv_norm, w_ukv, angles)
    y_mla_l = attend(q_l, jnp.concatenate([k_c, k_l], 1), jnp.concatenate([v_c, v_l], 1))
    fc = mlstm_features(xm_c, conv_w, conv_b, w_qblk, w_kblk, w_vblk, w_gate, b_gate)
    fl = mlstm_features(xm_l, conv_w, conv_b, w_qblk, w_kblk, w_vblk, w_gate, b_gate)
    hc, hl = mlstm_bidir(fc[:4], fl[:4])
    out_l = merge(y_mla_l, mlstm_readout(hl, z_l, fl[4], ml_norm, ml_skip), gmla_l, gml_l, w_out)
    if last:
        return None, out_l
    y_mla_c = attend(q_c, k_c, v_c)
    out_c = merge(y_mla_c, mlstm_readout(hc, z_c, fc[4], ml_norm, ml_skip), gmla_c, gml_c, w_out)
    return out_c, out_l

def ec_moe(x, w_router, w_e_gate, w_e_up, w_e_down):
    B, T, D = x.shape
    cap = CAP_FACTOR * T // N_EXPERTS
    aff = jax.nn.softmax((x @ w_router).astype(jnp.float32), axis=-1)
    g, idx = lax.top_k(aff.transpose(0, 2, 1), cap)
    xs = jax.vmap(lambda xb, ib: xb[ib])(x, idx)
    a = jnp.einsum('becd,edf->becf', xs, w_e_gate)
    u = jnp.einsum('becd,edf->becf', xs, w_e_up)
    y = jnp.einsum('becf,efd->becd', jax.nn.silu(a) * u, w_e_down) * g[..., None].astype(x.dtype)
    return jax.vmap(lambda yb, ib: jnp.zeros((T, D), x.dtype).at[ib.reshape(-1)].add(yb.reshape(-1, D)))(y, idx)

def second_inputs(seed: int = 0) -> dict:
    key = jax.random.key(seed)
    ks = jax.random.split(key, 32)
    f32 = jnp.float32
    nrm = lambda k, shape, fan: jax.random.normal(k, shape, f32) * (fan ** -0.5)
    gain = lambda k, shape: 1.0 + 0.02 * jax.random.normal(k, shape, f32)
    L, D = DEPTH_2, D_MODEL
    b_gate = (0.1 * jax.random.normal(ks[16], (L, 2, 2, ML_HEADS), f32)
              + jnp.array([0.0, 3.0], f32)[None, None, :, None]).reshape(L, 4 * ML_HEADS)
    return {
        "x": jax.random.normal(ks[0], (BATCH, SEQ, D), f32),
        "c": jax.random.normal(ks[1], (BATCH, D), f32),
        "ctx": jax.random.normal(ks[2], (BATCH, CTX_LEN, D), f32),
        "c_ctx": jax.random.normal(ks[3], (D,), f32),
        "w_mod": nrm(ks[4], (L, D, 6 * D), D) * 0.5,
        "b_mod": 0.02 * jax.random.normal(ks[5], (L, 6 * D), f32),
        "norm1": gain(ks[6], (L, D)),
        "w_in": nrm(ks[7], (L, D, IN_DIM), D),
        "q_norm": gain(ks[8], (L, Q_LORA)),
        "w_uq": nrm(ks[9], (L, Q_LORA, MLA_HEADS * (QK_NOPE + QK_ROPE)), Q_LORA),
        "kv_norm": gain(ks[10], (L, KV_LORA)),
        "w_ukv": nrm(ks[11], (L, KV_LORA, MLA_HEADS * (QK_NOPE + V_DIM)), KV_LORA),
        "conv_w": nrm(ks[12], (L, CONV_W, ML_INNER), CONV_W),
        "conv_b": 0.02 * jax.random.normal(ks[13], (L, ML_INNER), f32),
        "w_qblk": nrm(ks[14], (L, QKV_NBLK, QKV_BLOCK, QKV_BLOCK), QKV_BLOCK),
        "w_kblk": nrm(ks[15], (L, QKV_NBLK, QKV_BLOCK, QKV_BLOCK), QKV_BLOCK),
        "w_vblk": nrm(ks[17], (L, QKV_NBLK, QKV_BLOCK, QKV_BLOCK), QKV_BLOCK),
        "w_gate": nrm(ks[18], (L, 3 * ML_INNER, 4 * ML_HEADS), 3 * ML_INNER) * 0.5,
        "b_gate": b_gate,
        "ml_norm": gain(ks[19], (L, ML_INNER)),
        "ml_skip": gain(ks[20], (L, ML_INNER)),
        "w_out": nrm(ks[21], (L, D, D), D),
        "norm2": gain(ks[22], (L, D)),
        "w_router": nrm(ks[23], (L, D, N_EXPERTS), D),
        "w_e_gate": nrm(ks[24], (L, N_EXPERTS, D, EXPERT_FF), D),
        "w_e_up": nrm(ks[25], (L, N_EXPERTS, D, EXPERT_FF), D),
        "w_e_down": nrm(ks[26], (L, N_EXPERTS, EXPERT_FF, D), EXPERT_FF),
        "final_norm": gain(ks[27], (D,)),
    }

def second_block(x, c, ctx, c_ctx, w_mod, b_mod, norm1, w_in, q_norm, w_uq, kv_norm, w_ukv, conv_w, conv_b,
              w_qblk, w_kblk, w_vblk, w_gate, b_gate, ml_norm, ml_skip, w_out, norm2, w_router,
              w_e_gate, w_e_up, w_e_down, final_norm):
    angles = axial_angles(x.shape[1])
    for l in range(DEPTH_2):
        last = l == DEPTH_2 - 1
        mod_l = jax.nn.silu(c) @ w_mod[l] + b_mod[l]
        mod_c = jax.nn.silu(c_ctx)[None, :] @ w_mod[l] + b_mod[l]
        sh1, sc1, g1, sh2, sc2, g2 = jnp.split(mod_l, 6, axis=-1)
        sh1c, sc1c, g1c, sh2c, sc2c, g2c = jnp.split(mod_c, 6, axis=-1)
        h_l = modulate(rmsnorm(x, norm1[l]), sh1, sc1)
        h_c = modulate(rmsnorm(ctx, norm1[l]), sh1c, sc1c)
        out_c, out_l = mixer(h_c, h_l, angles, last, w_in[l], q_norm[l], w_uq[l], kv_norm[l], w_ukv[l],
                             conv_w[l], conv_b[l], w_qblk[l], w_kblk[l], w_vblk[l], w_gate[l], b_gate[l],
                             ml_norm[l], ml_skip[l], w_out[l])
        x = x + g1[:, None, :] * out_l
        h_l = modulate(rmsnorm(x, norm2[l]), sh2, sc2)
        x = x + g2[:, None, :] * ec_moe(h_l, w_router[l], w_e_gate[l], w_e_up[l], w_e_down[l])
        if not last:
            ctx = ctx + g1c[:, None, :] * out_c
            h_c = modulate(rmsnorm(ctx, norm2[l]), sh2c, sc2c)
            ctx = ctx + g2c[:, None, :] * ec_moe(h_c, w_router[l], w_e_gate[l], w_e_up[l], w_e_down[l])
    return rmsnorm(x, final_norm)


def setup_inputs(seed=0):
    out = dict(first_inputs(seed))
    for name, value in second_inputs(seed + 1).items():
        if name != "x":
            out[name + "_2"] = value
    return out


def reference(
    x, mem, norm_mix, w_in, w_proj_a, w_proj_b, w_proj_m, w_out, norm_mem, w_mem_kv, norm_mlp,
    w_up, w_down, norm_final, c_2, ctx_2, c_ctx_2, w_mod_2, b_mod_2, norm1_2, w_in_2, q_norm_2,
    w_uq_2, kv_norm_2, w_ukv_2, conv_w_2, conv_b_2, w_qblk_2, w_kblk_2, w_vblk_2, w_gate_2,
    b_gate_2, ml_norm_2, ml_skip_2, w_out_2, norm2_2, w_router_2, w_e_gate_2, w_e_up_2,
    w_e_down_2, final_norm_2,
):
    x = first_block(
        x, mem, norm_mix, w_in, w_proj_a, w_proj_b, w_proj_m, w_out, norm_mem, w_mem_kv,
        norm_mlp, w_up, w_down, norm_final,
    )
    return second_block(
        x, c_2, ctx_2, c_ctx_2, w_mod_2, b_mod_2, norm1_2, w_in_2, q_norm_2, w_uq_2, kv_norm_2,
        w_ukv_2, conv_w_2, conv_b_2, w_qblk_2, w_kblk_2, w_vblk_2, w_gate_2, b_gate_2,
        ml_norm_2, ml_skip_2, w_out_2, norm2_2, w_router_2, w_e_gate_2, w_e_up_2, w_e_down_2,
        final_norm_2,
    )


_drawn_inputs = setup_inputs


def setup_inputs(seed=0):
    import zlib

    import numpy as np

    out = dict(_drawn_inputs(seed))
    spreads = {}
    factors = {'norm_mix': 2.823,
     'norm_mem': 8.0,
     'ctx_2': 3.395,
     'b_mod_2': 3.679,
     'norm1_2': 8.0,
     'q_norm_2': 8.0,
     'w_uq_2': 3.277,
     'kv_norm_2': 8.0,
     'conv_b_2': 8.0,
     'w_gate_2': 2.681,
     'ml_norm_2': 47.966,
     'ml_skip_2': 8.0,
     'norm2_2': 8.0,
     'final_norm_2': 7.953}
    for name, (base, spread) in spreads.items():
        noise = np.random.default_rng([zlib.crc32(name.encode()), seed]).standard_normal(out[name].shape)
        drawn = base * np.exp(spread * noise) if base else spread * noise
        out[name] = jnp.asarray(drawn.astype(out[name].dtype))
    for name, factor in factors.items():
        out[name] = (out[name] * factor).astype(out[name].dtype)
    return out
```

```python
from contextlib import ExitStack

import numpy as np

import concourse.bass as bass
from concourse import mybir

ALU = mybir.AluOpType
ACT = mybir.ActivationFunctionType
F32 = mybir.dt.float32
F32R = mybir.dt.float32r
U32 = mybir.dt.uint32
AX_X = mybir.AxisListType.X

P = 128
D = 1024
T = 256
TT = T // P
KC = D // P
EPS = 1e-6
NEG = -1e30

DEPTH = 2
HD = 64
DILATIONS = (1, 4, 16)
WA, WB, WM = 384, 384, 256
D_IN = 3 * WA + 3 * WB + WM + 3 * D
COL_QM = 3 * WA + 3 * WB
COL_GATE = COL_QM + WM
FF = 4 * D

H2, NOPE, PE2, VD = 8, 128, 64, 128
QL, KVL = 384, 256
SCALE2 = (NOPE + PE2) ** -0.5
IN2 = QL + KVL + PE2 + 4 * D
MH, MD = 4, 256
TAPS = 5
NE, CAP = 16, 32
EG = 4

R = 8
UC, UN = 4, 512
UNITS1 = 64
R1 = 4
SPLIT = [u for u in range(2, UNITS1) if not 24 <= u < 28]
LO_VECTOR = [4, 6, 8, 10] + list(range(34, UNITS1, 2))
LO_POOL = [u for u in SPLIT if u not in LO_VECTOR]


def constants():
    p = np.arange(P)[:, None]
    c = np.arange(P)[None, :]
    parts = {}
    parts["ident"] = np.eye(P)
    far = {1: c >= p, 4: (P + p - c) % 4 == 0, 16: (P + p - c) % 16 == 0}
    bands = []
    for dil in DILATIONS:
        bands += [far[dil], (c <= p) & ((p - c) % dil == 0)]
    parts["dilated"] = np.where(np.concatenate(bands, 1), 0.0, NEG)
    parts["causal"] = np.concatenate([np.zeros((P, 2 * P)), np.where(c <= p, 0.0, NEG)], 1)
    pos = np.arange(T, dtype=np.float32)
    inv = (1.0 / (np.float32(500000.0) ** (np.arange(0, 16, 2, dtype=np.float32) / np.float32(16)))).astype(np.float32)
    ang = pos[:, None] * inv[None, :]
    cos, sin = np.cos(ang), np.sin(ang)
    tiles = lambda a: a.reshape(TT, P, -1).transpose(1, 0, 2).reshape(P, -1)
    parts["cos1"] = tiles(np.concatenate([cos, cos], 1))
    parts["sin1"] = tiles(np.concatenate([-sin, sin], 1))
    inv2 = (np.float32(10000.0) ** (-np.arange(16, dtype=np.float32) / np.float32(16))).astype(np.float32)
    row = (np.arange(T) // 64).astype(np.float32)[:, None] * inv2
    col = (np.arange(T) % 64).astype(np.float32)[:, None] * inv2
    parts["cos2"] = tiles(np.concatenate([np.cos(row)] * 2 + [np.cos(col)] * 2, 1))
    parts["sin2"] = tiles(np.concatenate([-np.sin(row), np.sin(row), -np.sin(col), np.sin(col)], 1))
    parts["before"] = np.where(p <= c, 0.0, -NEG)
    parts["after"] = np.where(p >= c, 0.0, -NEG)
    for name, kind in (("sel_i", 0), ("sel_f", 1)):
        m = np.zeros((P, 8))
        for j in range(4):
            for d in range(2):
                for h in range(4):
                    m[32 * j + d * 8 + kind * 4 + h, d * 4 + h] = 1.0
        parts[name] = m
    parts["iota"] = np.broadcast_to(np.arange(T)[None, :], (P, T))
    parts["token"] = p + P * np.arange(TT)[None, :]
    parts["block4"] = (np.arange(32)[None, :] == p // 4)
    parts["one"] = np.ones((P, 1))
    at, n = {}, 0
    for k, a in parts.items():
        at[k] = (n, a.shape[1])
        n += a.shape[1]
    return at, np.ascontiguousarray(np.concatenate([np.asarray(a, np.float32) for a in parts.values()], 1))


def attention_jobs():
    jobs = []
    for h in range(2):
        for t in range(TT):
            blocks = [(g, 3 + g, kt, ("z", 2 * WA + HD * (2 * g + h))) for g in range(3) for kt in range(t + 1)]
            jobs.append(dict(kind="dilated", t=t, base=HD * h, blocks=blocks, out=0))
    for h in range(6):
        for t in range(TT):
            blocks = [(6 + h // 2, 9 + h // 2, kt, ("z", 3 * WA + 2 * WB + HD * h)) for kt in range(t + 1)]
            jobs.append(dict(kind="causal", t=t, base=HD * (h % 2), blocks=blocks, out=1 + h // 2))
    for h in range(4):
        for t in range(TT):
            blocks = [(12 + h // 2, h // 2, kt, ("mem", WM + HD * h)) for kt in range(TT)]
            jobs.append(dict(kind="memory", t=t, base=HD * (h % 2), blocks=blocks, out=4 + h // 2))
    return jobs


JOBS = attention_jobs()
NJ = len(JOBS)


def z_column(chunk):
    return P * chunk if chunk < 6 else (3 * WA + P * (chunk - 6) if chunk < 12 else COL_QM + P * (chunk - 12))


ROWS2 = []
for _name, _n in (("c_2", 8), ("c_ctx_2", 8), ("norm1_2", 8), ("norm2_2", 8), ("q_norm_2", 3), ("kv_norm_2", 2),
                  ("conv_w_2", 40), ("conv_b_2", 8), ("ml_skip_2", 8)):
    ROWS2.append((_name, sum(r[2] for r in ROWS2), _n))
N_ROWS2 = sum(r[2] for r in ROWS2)
N_CONST = 4 + len(ROWS2)


def rows_of(a):
    names = " ".join("abcd"[:len(a.shape) - 1])
    return a.rearrange(f"{names} (k p) -> ({names} k) p", p=P)


_XM, _Z, _GA, _GM = QL + KVL + PE2, QL + KVL + PE2 + D, QL + KVL + PE2 + 2 * D, QL + KVL + PE2 + 3 * D
IN_TILES = [(0, QL), (QL, KVL + PE2), (_XM, UN), (_Z, UN), (_XM + UN, UN), (_Z + UN, UN),
            (_GM, UN), (_GM + UN, UN), (_GA, UN), (_GA + UN, UN)]

U_IN = DEPTH * UNITS1
U8 = U_UQ = U_IN + 2 * len(IN_TILES)
U_UKV, U_OUT, U_EX = U_UQ + 4, U_UQ + 8, U_UQ + 12


RE = R + 4


def ring_slot(u):
    if u < U8:
        return u % R1
    if u < U_EX:
        return (u - U8) % R
    i = (u - U_EX) % RE
    return (i + 4) % R if i < R else i


def build(nc, w, out):
    at, _ = constants()
    start = {}
    with ExitStack() as ctx:
        def sb(name, shape, dt=F32):
            start[name] = (nc.sbuf_base + 31) // 32 * 32
            return ctx.enter_context(nc.sbuf_tensor(name, shape, dt))

        def in_place(name, of, first, shape):
            return nc.alloc_sbuf_tensor_at(name, [P] + shape, F32R, offset=start[of] + 4 * first)

        def sem(name):
            return ctx.enter_context(nc.semaphore(name))

        arena = sb("arena", [P, 27600])
        ring = sb("ring", [P, R, UC, UN])
        x = sb("x", [P, TT, D])
        xn = sb("xn", [P, TT, D])
        hT = sb("hT", [P, KC, T])
        consts = sb("consts", [P, sum(n for _, n in at.values())])
        rows1 = arena[0:48, 26880:27008]
        rows2 = arena[0:N_ROWS2, 27008:27136]
        cols = sb("cols", [P, 48 + N_ROWS2])
        g_feat = cols[:, 0:48].rearrange("p (i l c) -> p i l c", i=3, l=DEPTH)
        col2 = {name: cols[:, 48 + a:48 + a + n] for name, a, n in ROWS2}
        silu_c = sb("silu_c", [P, DEPTH, UC, 32])
        g_now = sb("g_now", [P, 3, KC])
        stat = sb("stat", [P, 2, 4])
        mx = sb("mx", [P, NJ])
        nmx = sb("nmx", [P, NJ])
        den = sb("den", [P, NJ])
        rden = sb("rden", [P, NJ])

        def const(name):
            a, n = at[name]
            return consts[:, a:a + n]

        def carve(first, *dims):
            n = int(np.prod(dims))
            v = arena[:, first:first + n]
            if len(dims) == 2:
                v = v.rearrange("p (a b) -> p a b", a=dims[0])
            if len(dims) == 3:
                v = v.rearrange("p (a b c) -> p a b c", a=dims[0], b=dims[1])
            return v

        ident = const("ident")
        z = carve(0, TT, D_IN)
        qkT = carve(11264, 14, T)
        memnT = carve(21760, KC, T)
        kv_mem = carve(14848, TT, 2 * WM)
        kmT = carve(15872, 2, T)
        S = carve(16384, 3, 768)
        memT = carve(16384, KC, T)
        PT = carve(18688, 2, 6, P)
        rope_a = carve(18688, TT, 384)
        rope_b = carve(19456, TT, 384)
        oT = carve(20224, 6, T)
        mod_acc = carve(25856, 3, UN)
        silu_now = carve(27392, UC, 32)
        mod_slot = [carve(16384, UC, UN), carve(18432, UC, UN), xn[:, :, :].rearrange("p t (c n) -> p (t c) n", n=UN),
                    hT[:, :, :].rearrange("p k t -> p (k t)").rearrange("p (c n) -> p c n", n=UN)]
        r_up = carve(18432, 2, TT, UN)
        hT_hi = in_place("hT_hi", "hT", 0, [KC, T])
        hT_lo = in_place("hT_lo", "arena", 23808, [KC, T])
        uT_hi = in_place("uT_hi", "arena", 0, [FF // P, T])
        uT_lo = in_place("uT_lo", "arena", 8192, [FF // P, T])
        ring_lo = in_place("ring_lo", "ring", 0, [R1, UC, UN])
        ring_hi = in_place("ring_hi", "ring", R1 * UC * UN, [R1, UC, UN])

        psum = ctx.enter_context(nc.psum_tensor("psum", [P, 8, UN], F32))
        DB = [psum[:, 2 * i:2 * i + 2, :] for i in range(4)]
        flat = [d.rearrange("p a b -> p (a b)") for d in DB]

        const_in = sem("const_in")
        cols_full = sem("cols_full")
        cols_sb = sem("cols_sb")
        x_in = sem("x_in")
        mem_in = sem("mem_in")
        slot_in = [sem(f"slot_in{i}") for i in range(R)]
        hi_sb = sem("hi_sb")
        lo_v = sem("lo_v")
        lo_p = sem("lo_p")
        slots_free = sem("slots_free")
        norm_a = sem("norm_a")
        norm_v = sem("norm_v")
        turn_full = sem("turn_full")
        turn_v = sem("turn_v")
        turn_a = sem("turn_a")
        turn_lo = sem("turn_lo")
        gains = sem("gains")
        mem_g = sem("mem_g")
        kv_sb = sem("kv_sb")
        km_full = sem("km_full")
        km_sb = sem("km_sb")
        z_sb = sem("z_sb")
        rope_s = sem("rope_s")
        qk_full = sem("qk_full")
        qk_sb = sem("qk_sb")
        s_full = sem("s_full")
        s_seen = sem("s_seen")
        s_v = sem("s_v")
        e_sb = sem("e_sb")
        p_v = sem("p_v")
        t_full = sem("t_full")
        t_sb = sem("t_sb")
        o_full = sem("o_full")
        o_sb = sem("o_sb")
        g_exp = sem("g_exp")
        g_one = sem("g_one")
        g_rec = sem("g_rec")
        pa_full = sem("pa_full")
        pj_sb = sem("pj_sb")
        y_sum = sem("y_sum")
        wo_x = sem("wo_x")
        relu_sb = sem("relu_sb")
        up_sb = sem("up_sb")
        u_full = sem("u_full")
        u_sb = sem("u_sb")
        u_lo = sem("u_lo")
        dn_x = sem("dn_x")
        bias_in = sem("bias_in")
        zeros = sem("zeros")
        silu_sb = sem("silu_sb")
        silu_l = sem("silu_l")
        mod_in = sem("mod_in")
        mod_full = sem("mod_full")
        mod_add = sem("mod_add")
        x_ready = sem("x_ready")
        fin_v = sem("fin_v")
        out_done = sem("out_done")

        ctx_x = carve(23808, TT, D)
        ctx_n = carve(13888, TT, D)
        final_row = carve(21760, D)
        modrow = carve(0, 3, UN)
        xm = carve(1536, KC, 2, T + 4)
        gated = carve(5696, TT, D)
        zg = carve(7744, TT, D)
        hT2 = carve(9792, KC, 2 * T)
        hT2_lo = in_place("hT2_lo", "arena", 9792, [KC, 2 * T])
        hT2_hi = in_place("hT2_hi", "arena", 17984, [KC, 2 * T])
        k_tok = carve(9792, 4, H2, NOPE)
        v_tok = carve(13888, 4, H2, VD)
        q_lat = carve(13888, TT, QL)
        kv_lat = carve(14656, 4, KVL + PE2)
        xm_tok = carve(15936, 4, UN)
        kT2 = carve(17984, H2, 2 * T)
        q_tok = carve(17984, TT, H2 * (NOPE + PE2))
        qpT = carve(22080, 4, T)
        kpT = carve(23104, 2 * T)
        prob = carve(23616, 2, UN)
        probT = carve(24640, 2, 4, P)
        q_pe = carve(23616, TT, H2 * PE2)
        k_pe = carve(24640, 4, 2 * PE2)
        gate_tmp = carve(23616, 2, TT, UN)
        qlT = carve(25664, 3, T)
        kvlT = carve(26432, 2, 2 * T)
        xn_flat = xn[:, :, :].rearrange("p t d -> p (t d)")
        hT_flat = hT[:, :, :].rearrange("p k t -> p (k t)")
        xc = carve(9792, KC, 2, T)
        vF = carve(9792, KC, 2 * T)
        decays = [carve(9792, 2, 4, T), carve(3648, 2, 4, T)]
        h_tok = carve(11840, TT, D)
        qkF = carve(13888, 2, KC, 2 * T)
        v_ml = carve(22080, 4, MH, MD + 1)
        bd = [xn_flat[:, 0:1024], xn_flat[:, 1024:2048], carve(26192, KC * P)]
        bd = [b.rearrange("p (c n) -> p c n", c=KC) for b in bd]
        wg = carve(27216, 24, 16)
        skipped = hT
        gp = hT_flat[:, 0:UN]
        skip_tmp = carve(22080, TT, D)
        ml_row = carve(2048, D)
        masked = carve(3072, 2, TT, P)
        junk = carve(1536, MD)
        gi, Ff, lf, Fb = [xn_flat[0:8, UN * i:UN * (i + 1)] for i in range(4)]
        af, ab, Gf, Gb = [hT_flat[0:8, UN * i:UN * (i + 1)] for i in range(4)]
        more_slots = [carve(1536 + UC * UN * i, UC, UN) for i in range(RE - R)]
        xsT = carve(9792, KC, NE * CAP)
        stage = carve(13888, KC, P)
        pick = carve(14912, TT, NE * CAP)
        pickT = carve(15936, EG, T)
        wide = carve(16960, 2, NE, CAP)
        hid = carve(17984, 2, UN)
        hid_u = carve(19008, D)
        hidT = carve(20032, KC, P)
        y_ex = carve(21056, EG, D)
        g_row = carve(25152, D)
        last_row = carve(26176, D)
        x_tmp = carve(13888, TT, UN)

        small = consts[:, at["dilated"][0]:at["dilated"][0] + 1152]
        def piece(first, *dims):
            n = int(np.prod(dims))
            v = small[:, first:first + n]
            if len(dims) == 2:
                v = v.rearrange("p (a b) -> p a b", a=dims[0])
            if len(dims) == 3:
                v = v.rearrange("p (a b c) -> p a b c", a=dims[0], b=dims[1])
            return v

        modT = piece(700, 48, 2)
        amp1 = piece(256, KC, 2)
        amp2 = piece(272, KC, 1)
        lat = piece(280, 4, 6)
        mx2, nmx2, den2, rden2 = [piece(304 + 16 * i, 16) for i in range(4)]
        blk = piece(368, 3, KC, 4)
        b_if = piece(464, 2)
        aT = piece(468, 2, 4, 8)
        em = piece(532, 2, TT, 4)
        dens = piece(564, 4, 4)
        hst = piece(580, 4, 8)
        aff = piece(612, TT, NE)
        rst = piece(644, 4, TT)
        wr = piece(0, KC, 16)
        top = piece(796, CAP)[0:NE, :]
        topi = piece(828, CAP)[0:NE, :].bitcast(U32)
        topf = piece(860, CAP)[0:NE, :]
        affT = piece(892, T)[0:NE, :]
        slotT = piece(652, 2, EG, 1)

        row_in = sem("row_in")
        quad_in = sem("quad_in")
        ctx_in = sem("ctx_in")
        x_row = sem("x_row")
        h2_parts = sem("h2_parts")
        modrow_sb = sem("modrow_sb")
        mt_full = sem("mt_full")
        mod_sb = sem("mod_sb")
        lat_sb = sem("lat_sb")
        xm_sb = sem("xm_sb")
        xt_full = sem("xt_full")
        xt_sb = sem("xt_sb")
        xm_pad = sem("xm_pad")
        gp_zero = sem("gp_zero")
        b_in = sem("b_in")
        sig_sb = sem("sig_sb")
        zg_sb = sem("zg_sb")
        lat_sq = sem("lat_sq")
        lat_root = sem("lat_root")
        lat_n = sem("lat_n")
        lt_full = sem("lt_full")
        ql_sb = sem("ql_sb")
        kvl_sb = sem("kvl_sb")
        kpe_sb = sem("kpe_sb")
        q_sb = sem("q_sb")
        kv_v = sem("kv_v")
        kv_a = sem("kv_a")
        qpe_sb = sem("qpe_sb")
        qt_full = sem("qt_full")
        qt_v = sem("qt_v")
        qt_a = sem("qt_a")
        s2_full = sem("s2_full")
        s2_v = sem("s2_v")
        e2_sb = sem("e2_sb")
        r2_v = sem("r2_v")
        t2_full = sem("t2_full")
        t2_sb = sem("t2_sb")
        y2_full = sem("y2_full")
        y2_sb = sem("y2_sb")
        conv_s = sem("conv_s")
        blk_in = sem("blk_in")
        bd_sb = sem("bd_sb")
        xc_sb = sem("xc_sb")
        qk2_full = sem("qk2_full")
        qk2_v = sem("qk2_v")
        qk2_a = sem("qk2_a")
        skip_sb = sem("skip_sb")
        sk_full = sem("sk_full")
        sk_v = sem("sk_v")
        vf_full = sem("vf_full")
        vf_sb = sem("vf_sb")
        wg_in = sem("wg_in")
        vt_full = sem("vt_full")
        vt_sb = sem("vt_sb")
        ones_sb = sem("ones_sb")
        gp_full = sem("gp_full")
        gp_sb = sem("gp_sb")
        gr_full = sem("gr_full")
        gr_v = sem("gr_v")
        gr_a = sem("gr_a")
        at_full = sem("at_full")
        at_sb = sem("at_sb")
        raw_full = sem("raw_full")
        dec_v = sem("dec_v")
        dec_a = sem("dec_a")
        w_v = sem("w_v")
        num_full = sem("num_full")
        h_v = sem("h_v")
        hn_a = sem("hn_a")
        mix_v = sem("mix_v")
        mlrow_in = sem("mlrow_in")
        gb_full = sem("gb_full")
        gb_sb = sem("gb_sb")
        x2_v = sem("x2_v")
        wr_in = sem("wr_in")
        lg_full = sem("lg_full")
        rt_v = sem("rt_v")
        rt_a = sem("rt_a")
        af_full = sem("af_full")
        top_v = sem("top_v")
        sl_full = sem("sl_full")
        sl_v = sem("sl_v")
        xs_full = sem("xs_full")
        xs_v = sem("xs_v")
        xs_a = sem("xs_a")
        stage_sb = sem("stage_sb")
        hid_a = sem("hid_a")
        hid_v = sem("hid_v")
        ht_full = sem("ht_full")
        ht_sb = sem("ht_sb")
        ye_sb = sem("ye_sb")
        sc_full = sem("sc_full")
        fin_row_in = sem("fin_row_in")
        TURN = 1 + 9 * DEPTH
        FULL = 2 + 6 * DEPTH

        def slot(u):
            s = ring_slot(u)
            return ring[:, s, :, :] if s < R else more_slots[s - R]

        def landed(u):
            return slot_in[ring_slot(u)] if ring_slot(u) < R else quad_in

        def slot_hi(u):
            return ring_hi[:, u % R1, :, :]

        def slot_lo(u):
            return ring_lo[:, u % R1, :, :]

        def unit_done(u):
            return R1 + u + 1

        def split_hi(act, l, u):
            act.wait_ge(slot_in[u % R1], l * (UNITS1 // R1) * 16 + 16 * (u // R1 + 1))
            act.wait_ge(slots_free, l * UNITS1 + unit_done(u - R1))
            act.activation(slot_hi(u), slot(u), ACT.Copy).then_inc(hi_sb, 1)

        def split2_hi(act, i):
            u, n = U_IN + i, IN_TILES[i // 2][1]
            act.wait_ge(slot_in[u % R1], 16 * (u // R1 + 1))
            act.wait_ge(slots_free, unit_done(u - R1))
            act.activation(slot_hi(u)[:, :, 0:n], slot(u)[:, :, 0:n], ACT.Copy).then_inc(hi_sb, 1)

        def split2_lo(pool, i):
            u, n = U_IN + i, IN_TILES[i // 2][1]
            pool.wait_ge(hi_sb, DEPTH * len(SPLIT) + i + 1)
            pool.tensor_tensor(slot_lo(u)[:, :, 0:n], slot(u)[:, :, 0:n], slot_hi(u)[:, :, 0:n].bitcast(F32), ALU.subtract)\
                .then_inc(lo_p, 1)

        def split_lo(eng, l, u):
            eng.wait_ge(hi_sb, l * len(SPLIT) + SPLIT.index(u) + 1)
            mine, done = (LO_VECTOR, lo_v) if u in LO_VECTOR else (LO_POOL, lo_p)
            eng.tensor_tensor(slot_lo(u), slot(u), slot_hi(u).bitcast(F32), ALU.subtract).then_inc(done, 1)

        block = ctx.enter_context(nc.Block())

        def chunks(a):
            return a.rearrange("(c p) n -> p c n", p=P)

        def layer_units(l):
            mkv, win, wpj = w["w_mem_kv"], w["w_in"], w["w_proj"]
            wo, up, dn = w["w_out"], w["w_up"], w["w_down"]
            src = [chunks(mkv[l, UN * kh:UN * kh + UN, :]) for kh in range(2)]
            src += [chunks(win[l, UN * kh:UN * kh + UN, UN * n:UN * n + UN]) for n in range(11) for kh in range(2)]
            for n in range(2):
                src += [chunks(wpj[l, 0:512, UN * n:UN * n + UN]), chunks(wpj[l, 512:768, UN * n:UN * n + UN])]
            src += [chunks(wo[l, UN * kh:UN * kh + UN, UN * n:UN * n + UN]) for n in range(2) for kh in range(2)]
            src += [chunks(up[l, UN * kh:UN * kh + UN, UN * n:UN * n + UN]) for n in range(8) for kh in range(2)]
            src += [chunks(dn[l, UN * kg:UN * kg + UN, UN * n:UN * n + UN]) for kg in range(8) for n in range(2)]
            assert len(src) == UNITS1
            return src

        def sync_block2(sp, load):
            sp.dma_start(final_row, w["norm_final"].partition_broadcast(P)).then_inc(row_in, 16)
            win, wuq, wukv, wout = (w[n][0] for n in ("w_in_2", "w_uq_2", "w_ukv_2", "w_out_2"))

            def columns(a, c0, n):
                return [chunks(a[UN * kh:UN * kh + UN, c0:c0 + n]) for kh in range(2)]

            src = []
            for c0, n in IN_TILES:
                src += columns(win, c0, n)
            src += [chunks(wuq[:, 384 * n:384 * n + 384]) for n in range(4)]
            src += [chunks(wukv[:, UN * n:UN * n + UN]) for n in range(4)]
            for n in range(2):
                src += columns(wout, UN * n, UN)
            assert U_IN + len(src) == U_EX
            for i, s in enumerate(src):
                load(U_IN + i, s, unit_done(U_IN + i - (R1 if U_IN + i < U8 + R1 else R)))

            def expert_unit(i, g):
                name, n, kh, j = ("w_e_gate_2", "w_e_up_2", "w_e_down_2")[i % 48 // 16], i // 8 % 2, i // 4 % 2, i % EG
                groups = w[name][0].rearrange("(g e) a b -> g e a b", e=EG)[i // 48:]
                return chunks(groups[g, j, UN * kh:UN * kh + UN, UN * n:UN * n + UN])

            for i in range(RE):
                load(U_EX + i, expert_unit(i, 0), unit_done(U_EX + i - (R if i < R else RE)))
            with sp.Fori(0, NE // EG - 1) as g:
                for i in range(RE, RE + 48):
                    load(U_EX + i, expert_unit(i, g), g * 48 + unit_done(U_EX + i - RE), seen=i == 16)
            for i in range(RE, 48):
                load(U_EX + i, expert_unit(i, NE // EG - 1), (NE // EG - 1) * 48 + unit_done(U_EX + i - RE))
            sp.wait_ge(fin_v, 2)
            sp.dma_start(out.rearrange("b (t p) d -> p (b t) d", p=P), xn[:, :, :]).then_inc(out_done, 16)
            sp.wait_ge(out_done, 16)

        def tensor_block2(pe, unit_ready, product, tokens, tile_of, to_features, split_product):
            def banks(outs, a, u, n, kc=KC):
                for kh in range((kc + UC - 1) // UC):
                    unit_ready(u + kh)
                    nk = min(UC, kc - UC * kh)
                    for b, t in outs:
                        last = product(psum[:, b, 0:n], tokens(a, t), UC * kh, u + kh, nk=nk, n=n, start=kh == 0,
                                       stop=UC * kh + nk == kc)
                    last.then_inc(slots_free, 1)

            pe.wait_ge(modrow_sb, 1)
            for q in range(3):
                for i in range(4):
                    last = pe.transpose(psum[:, 4 + q, i * P:(i + 1) * P], modrow[:, q, i * P:(i + 1) * P], ident)
                last.then_inc(mt_full, 1)
            pe.wait_ge(mod_sb, 5)
            pe.wait_ge(norm_v, 5 * 7)
            to_features(xn)
            pe.wait_ge(turn_v, TURN + 4)
            pe.wait_ge(turn_a, TURN + 4)
            pe.wait_ge(norm_v, 5 * 8)
            to_features(ctx_n)

            pe.wait_ge(turn_v, TURN + 8)
            pe.wait_ge(turn_a, TURN + 8)
            outs = {0: ((0, 2), (1, 3)), 1: ((2, 0), (3, 1), (4, 2), (5, 3)), 2: ((6, 0), (7, 1), (0, 2), (1, 3)),
                    3: ((2, 2), (3, 3)), 4: ((0, 0), (1, 1), (2, 2), (3, 3)), 5: ((4, 2), (5, 3)), 6: ((2, 2), (3, 3)),
                    7: ((0, 2), (1, 3)), 8: ((2, 2), (3, 3)), 9: ((0, 2), (1, 3))}

            def input_tile(i):
                n = IN_TILES[i][1]
                pe.wait_ge(h2_parts, 8 if i else 4)
                for kh in range(2):
                    u = U_IN + 2 * i + kh
                    unit_ready(u)
                    for b, t in outs[i]:
                        last = split_product(psum[:, b, 0:n], tokens(hT2_hi, t), tokens(hT2_lo, t), UC * kh, u, n=n,
                                             start=kh == 0, stop=kh == 1)
                    last.then_inc(slots_free, 1)

            def xm_features(i, first):
                pe.wait_ge(xm_sb, 2 * i + 2)
                for c in range(4):
                    for t in range(4):
                        last = pe.transpose(psum[:, first[c], t * P:(t + 1) * P], xm_tok[:, t, c * P:(c + 1) * P], ident)
                    last.then_inc(xt_full, 1)

            input_tile(0)
            input_tile(1)
            pe.wait_ge(lat_sb, 1)
            input_tile(2)
            pe.wait_ge(lat_sb, 2)
            input_tile(3)
            pe.wait_ge(lat_sb, 3)
            xm_features(0, (4, 5, 6, 7))
            pe.wait_ge(sig_sb, 1)
            input_tile(4)
            pe.wait_ge(xt_sb, 2)
            input_tile(5)
            pe.wait_ge(xt_sb, 4)
            xm_features(1, (6, 7, 0, 1))
            input_tile(6)
            pe.wait_ge(sig_sb, 2)
            pe.wait_ge(lat_n, 6)
            for k in range(3):
                for t in range(TT):
                    last = pe.transpose(flat[2][:, k * T + t * P:k * T + (t + 1) * P], q_lat[:, t, k * P:(k + 1) * P], ident)
            last.then_inc(lt_full, 1)
            pe.wait_ge(xt_sb, 6)
            for k in range(2):
                for t in range(4):
                    last = pe.transpose(psum[:, 6 + k, t * P:(t + 1) * P], kv_lat[:, t, k * P:(k + 1) * P], ident)
            last.then_inc(lt_full, 1)
            pe.wait_ge(xt_sb, 8)
            input_tile(7)
            pe.wait_ge(sig_sb, 3)
            input_tile(8)
            pe.wait_ge(sig_sb, 4)
            input_tile(9)

            pe.wait_ge(ql_sb, 3)
            pe.wait_ge(sig_sb, 5)
            pe.wait_ge(kvl_sb, 2)
            for n, b in enumerate((2, 4, 6, 0)):
                if n == 3:
                    pe.wait_ge(sig_sb, 6)
                banks(((b, 0), (b + 1, 1)), qlT, U_UQ + n, 384, kc=3)
            for n in range(4):
                if n < 2:
                    pe.wait_ge(q_sb, 2 + 2 * n)
                else:
                    pe.wait_ge(kv_a, 2 * n - 2)
                    pe.wait_ge(kv_v, 2 * n - 2)
                c, x_ = ((2, 4), (6, 0))[n % 2]
                banks(((c, 0), (c + 1, 1), (x_, 2), (x_ + 1, 3)), kvlT, U_UKV + n, UN, kc=2)
            pe.wait_ge(kv_a, 6)
            pe.wait_ge(kv_v, 6)
            for half in range(2):
                for h in range(4 * half, 4 * half + 4):
                    for t in range(TT):
                        last = pe.transpose(flat[1 + half][:, (h % 4) * T + t * P:(h % 4) * T + (t + 1) * P],
                                            q_tok[:, t, 192 * h:192 * h + NOPE], ident)
                last.then_inc(qt_full, 1)
            pe.wait_ge(qpe_sb, 6)
            pe.wait_ge(kv_a, 8)
            for c in range(4):
                for t in range(TT):
                    last = pe.transpose(flat[3][:, c * T + t * P:c * T + (t + 1) * P], q_pe[:, t, c * P:(c + 1) * P], ident)
            last.then_inc(qt_full, 1)
            pe.wait_ge(kpe_sb, 7)
            pe.wait_ge(kv_v, 8)
            for t in range(4):
                last = pe.transpose(psum[:, 0, t * P:(t + 1) * P], k_pe[:, t, :], ident)
            last.then_inc(qt_full, 1)
            for i, db in enumerate((1, 2, 3, 0)):
                if i == 0:
                    pe.wait_ge(qt_a, 1)
                elif i == 1:
                    pe.wait_ge(qt_v, 1)
                elif i == 2:
                    pe.wait_ge(qt_a, 2)
                else:
                    pe.wait_ge(qt_v, 2)
                for h in range(2):
                    for t in range(4):
                        last = pe.transpose(DB[db][:, h, t * P:(t + 1) * P], k_tok[:, t, 2 * i + h, :], ident)
                last.then_inc(qt_full, 1)
            pe.wait_ge(qt_a, 4)
            pe.wait_ge(qt_v, 4)

            NJ2 = H2 * TT
            for j in range(NJ2 + 2):
                if j < NJ2:
                    h, t = j // TT, j % TT
                    if j >= 2:
                        pe.wait_ge(e2_sb, j - 1)
                    base = 64 * (h % 2)
                    pe.matmul(psum[:, j % 2, :], hT[:, h, t * P:(t + 1) * P], kT2[:, h, :], start=True, stop=False)
                    pe.matmul(psum[:, j % 2, :], qpT[base:base + 64, h // 2, t * P:(t + 1) * P], kpT[base:base + 64, :],
                              start=False, stop=True).then_inc(s2_full, 1)
                if 1 <= j <= NJ2:
                    i = j - 1
                    pe.wait_ge(e2_sb, i + 1)
                    if i >= 2:
                        pe.wait_ge(t2_sb, i - 1)
                    for b in range(4):
                        last = pe.transpose(psum[:, 2 + i % 2, b * P:(b + 1) * P], prob[:, i % 2, b * P:(b + 1) * P], ident)
                    last.then_inc(t2_full, 1)
                if j >= 2:
                    i = j - 2
                    pe.wait_ge(t2_sb, i + 1)
                    if i >= 2:
                        pe.wait_ge(y2_sb, i - 1)
                    for b in range(4):
                        last = pe.matmul(psum[:, 4 + i % 2, 0:VD], probT[:, i % 2, b, :], v_tok[:, b, i // TT, :],
                                         start=b == 0, stop=b == 3)
                    last.then_inc(y2_full, 1)

            pe.wait_ge(bd_sb, 3)
            pe.wait_ge(y2_sb, NJ2)
            for c in range(KC):
                pe.wait_ge(xc_sb, c // 2 + 1)
                if c >= 4:
                    pe.wait_ge((qk2_v, qk2_a)[c % 2], (c - 4) // 2 + 1)
                for i in range(2):
                    last = pe.matmul(DB[c % 4][:, i, :], bd[i][:, c, :], xc[:, c, :, :], start=True, stop=True)
                last.then_inc(qk2_full, 1)
            pe.wait_ge(skip_sb, 2)
            for t in range(TT):
                pe.wait_ge((qk2_v, qk2_a)[t], 3)
                for c in range(KC):
                    last = pe.transpose(flat[t][:, c * P:(c + 1) * P], skipped[:, c, t * P:(t + 1) * P], ident)
                last.then_inc(sk_full, 1)
            for i in range(4):
                if i < 2:
                    pe.wait_ge((qk2_v, qk2_a)[i], 4)
                else:
                    pe.wait_ge(vf_sb, i - 1)
                for c in (2 * i, 2 * i + 1):
                    last = pe.matmul(DB[2 + i % 2][:, c % 2, :], bd[2][:, c, :], xm[:, c, :, 2:2 + T], start=True, stop=True)
                last.then_inc(vf_full, 1)
            pe.wait_ge(wg_in, 16)
            pe.wait_ge(vf_sb, 4)
            feats = [qkF[:, 0, c, :] for c in range(KC)] + [qkF[:, 1, c, :] for c in range(KC)] + [vF[:, c, :] for c in range(KC)]
            for i in range(6):
                for j in range(4):
                    last = pe.matmul(psum[32 * j:32 * j + 16, 4, :], wg[:, 4 * i + j, :], feats[4 * i + j], start=i == 0, stop=i == 5)
            last.then_inc(gp_full, 1)

            def values(t):
                pe.wait_ge(sk_v, 4)
                if t >= 2:
                    pe.wait_ge(vt_sb, t - 1)
                for c in range(KC):
                    f = 2 + P * (t % 2)
                    last = pe.matmul(flat[t % 2][:, c * P:(c + 1) * P], xm[:, c, t // 2, f:f + P], bd[2][:, c, :],
                                     start=True, stop=True)
                last.then_inc(vt_full, 1)

            values(0)
            pe.wait_ge(gp_sb, 4)
            pe.matmul(psum[0:8, 6, :], const("sel_i"), gp, start=True, stop=True)
            pe.matmul(psum[0:8, 7, :], const("sel_f"), gp, start=True, stop=True).then_inc(gr_full, 1)
            for t in range(1, 4):
                values(t)
            pe.wait_ge(gr_v, 14)
            for d in range(2):
                for t in range(4):
                    pe.transpose(psum[:, 4, 32 * d + 8 * t:32 * d + 8 * t + 8], (af, ab)[d][:, t * P:(t + 1) * P], ident[0:8, 0:8])
            for d in range(2):
                for t in range(TT):
                    c0 = 64 + 16 * d + 8 * t
                    last = pe.transpose(psum[:, 4, c0:c0 + 8], lf[:, d * T + t * P:d * T + (t + 1) * P], ident[0:8, 0:8])
            last.then_inc(at_full, 1)
            pe.wait_ge(vt_sb, 4)
            pe.wait_ge(ones_sb, 1)
            pe.wait_ge(at_sb, 3)
            def decay_rows(h):
                if h >= 2:
                    pe.wait_ge(dec_a, 10 * (h - 1))
                for d in range(2):
                    r = 4 * d + h
                    last = pe.matmul(psum[:, 2 + h % 2, d * T:(d + 1) * T], ident[0:8, r:r + 1].to_broadcast([8, P]),
                                     (Gf, Gb)[d][:, T:2 * T], start=True, stop=True)
                last.then_inc(raw_full, 1)

            def raw_scores(h):
                for s in range(4):
                    for k in range(2):
                        c = 2 * h + k
                        last = pe.matmul(flat[0][:, s * T:(s + 1) * T], qkF[:, 1, c, s * P:(s + 1) * P], qkF[:, 0, c, T:2 * T],
                                         start=k == 0, stop=k == 1)
                last.then_inc(raw_full, 1)

            decay_rows(0)
            raw_scores(0)
            for h in range(MH):
                if h + 1 < MH:
                    decay_rows(h + 1)
                pe.wait_ge(w_v, 4 * h + 4)
                if h + 1 < MH:
                    raw_scores(h + 1)
                if h:
                    pe.wait_ge(h_v, 8 * h)
                for d in range(2):
                    for t in range(TT):
                        src = [s for s in range(4) if s < 2 or (s - 2 <= t if d == 0 else s - 2 >= t)]
                        for s in src:
                            last = pe.matmul(psum[:, 4 + 2 * d + t, 0:MD + 1], decays[h % 2][:, d, s, t * P:(t + 1) * P],
                                             v_ml[:, s, h, :], start=s == src[0], stop=s == src[-1])
                last.then_inc(num_full, 1)

            def spread(q, j):
                for i in range(2):
                    col = ident[:, 32 * (j + i):32 * (j + i) + 1].to_broadcast([P, P])
                    last = pe.matmul(psum[:, 2 + i, :], col, modrow[:, q, :], start=True, stop=True)
                last.then_inc(gb_full, 1)

            pe.wait_ge(dec_a, 10 * MH)
            spread(1, 0)
            pe.wait_ge(h_v, 8 * MH)
            pe.wait_ge(mix_v, 12)
            to_features(gated)
            pe.wait_ge(turn_v, TURN + 9)
            pe.wait_ge(turn_a, TURN + 9)
            pe.wait_ge(gb_sb, 1)
            for n in range(2):
                tile_of(DB[n], hT, U_OUT + 2 * n, 0)
            pe.wait_ge(norm_v, 5 * 9)
            to_features(xn)
            pe.wait_ge(turn_v, TURN + 13)
            pe.wait_ge(turn_a, TURN + 13)
            pe.wait_ge(wr_in, 16)
            for t in range(TT):
                for k in range(KC):
                    last = pe.matmul(psum[:, 0, t * NE:(t + 1) * NE], hT[:, k, t * P:(t + 1) * P], wr[:, k, :],
                                     start=k == 0, stop=k == KC - 1)
            last.then_inc(lg_full, 1)
            spread(2, 2)
            pe.wait_ge(rt_v, 4)
            for t in range(TT):
                last = pe.transpose(psum[0:NE, 1, t * P:(t + 1) * P], aff[:, t, :], ident)
            last.then_inc(af_full, 1)
            pe.wait_ge(top_v, 16)
            one = const("one")
            pe.matmul(psum[:, 4, :], one[0:NE, :].to_broadcast([NE, P]), wide[0:NE, 0, :, :], start=True, stop=True)
            for kind in range(2):
                for g in range(4):
                    last = pe.matmul(psum[:, 5, 4 * kind + g:4 * kind + g + 1], wide[0:NE, kind, EG * g:EG * g + EG, :],
                                     one[0:NE, :], start=True, stop=True)
            last.then_inc(sl_full, 1)
            pe.wait_ge(sl_v, 7)
            pe.wait_ge(gb_sb, 2)
            for c in range(KC):
                for t in range(TT):
                    last = pe.matmul(psum[:, c, :], xn[:, t, c * P:(c + 1) * P], pick[:, t, :], start=t == 0, stop=t == 1)
                last.then_inc(xs_full, 1)
            pe.wait_ge(xs_v, 4)
            pe.wait_ge(xs_a, 4)
            with pe.Fori(0, NE // EG) as g:
                def experts(bank, lhsT, part):
                    for kh in range(2):
                        for k in range(UC):
                            for j in range(EG):
                                u = U_EX + 8 * part + 4 * kh + j
                                if k == 0:
                                    unit_ready(u, g)
                                mm = pe.matmul(psum[32 * j:32 * j + 32, bank, :], lhsT[:, UC * kh + k, 32 * j:32 * j + 32],
                                               slot(u)[:, k, :], start=kh == 0 and k == 0, stop=kh == 1 and k == UC - 1)
                                if k == UC - 1:
                                    mm.then_inc(slots_free, 1)

                pe.wait_ge(stage_sb, g + 1)
                for part in range(4):
                    experts(part, stage, part)
                pe.wait_ge(hid_v, g * 2 + 2)
                for k in range(KC):
                    last = pe.transpose(flat[2][:, k * P:(k + 1) * P], hid_u[:, k * P:(k + 1) * P], ident)
                last.then_inc(ht_full, 1)
                pe.wait_ge(ht_sb, g + 1)
                pe.wait_ge(ye_sb, g * 2 + 1)
                for n in range(2):
                    experts(6 + n, hidT, 4 + n)
            pe.wait_ge(ye_sb, 2 * (NE // EG) + 1)
            for n in range(2):
                for t in range(TT):
                    for g in range(4):
                        last = pe.matmul(DB[n][:, t, :], pickT[:, g, t * P:(t + 1) * P], y_ex[:, g, n * UN:(n + 1) * UN],
                                         start=g == 0, stop=g == 3)
                last.then_inc(sc_full, 1)

        def vector_block2(dve, norm):
            dve.wait_ge(mod_add, 3 * DEPTH + 1)
            dve.tensor_copy(modrow, mod_acc).then_inc(modrow_sb, 1)
            dve.wait_ge(row_in, 16)
            norm(5, x, xn)
            dve.wait_ge(norm_v, 5 * 6)
            dve.tensor_tensor(x[:, :, :], xn[:, :, :], final_row.unsqueeze(1).to_broadcast([P, TT, D]), ALU.mult).then_inc(x_row, 1)
            dve.wait_ge(x_row, 1)
            norm(6, x, xn)
            dve.wait_ge(ctx_in, 16)
            norm(7, ctx_x, ctx_n)

            for q in range(3):
                dve.wait_ge(mt_full, q + 1)
                v = psum[:, 4 + q, :].rearrange("p (i j m) -> p j i m", i=4, j=4)[:, :, :, 0:2]
                dve.tensor_copy(modT[:, 16 * q:16 * q + 16, :].rearrange("p (j i) m -> p j i m", j=4), v).then_inc(mod_sb, 1)
            dve.wait_ge(mod_sb, 3)
            dve.scalar_tensor_tensor(out=amp1, in0=modT[:, 8:16, :], scalar=1.0, op0=ALU.add, op1=ALU.mult,
                                     in1=col2["norm1_2"].unsqueeze(2).to_broadcast([P, KC, 2])).then_inc(mod_sb, 1)
            dve.scalar_tensor_tensor(out=amp2, in0=modT[:, 32:40, 0:1], scalar=1.0, op0=ALU.add, op1=ALU.mult,
                                     in1=col2["norm2_2"].unsqueeze(2)).then_inc(mod_sb, 1)
            dve.wait_ge(mod_sb, 5)

            def turn_modulated(full, dst, amp, shift):
                dve.wait_ge(turn_full, full)
                for k in range(4):
                    dve.tensor_scalar(dst[:, k, :], flat[2][:, k * T:(k + 1) * T], amp(k), shift(k), ALU.mult, ALU.add)\
                       .then_inc(turn_v, 1)

            for i, m in enumerate((0, 1)):
                turn_modulated(FULL + 1 + 2 * i, hT2[:, :, T * (1 - m):T * (2 - m)],
                               lambda k: amp1[:, k, m:m + 1], lambda k: modT[:, k, m:m + 1])
                for half in range(2):
                    dve.wait_ge((turn_v, turn_a)[half], TURN + 4 * i + 4)
                    v = lambda a: a[:, 4 * half:4 * half + 4, T * (1 - m):T * (2 - m)]
                    dve.tensor_copy(v(hT2_hi), v(hT2)).then_inc(h2_parts, 1)
                    dve.wait_ge(h2_parts, 4 * i + 2 * half + 1)
                    dve.tensor_tensor(v(hT2_lo), v(hT2), v(hT2_hi).bitcast(F32), ALU.subtract).then_inc(h2_parts, 1)

            dve.wait_ge(slots_free, unit_done(U_IN + 1))
            dve.tensor_copy(q_lat, psum[:, 0:2, 0:QL]).then_inc(lat_sb, 1)
            dve.wait_ge(slots_free, unit_done(U_IN + 3))
            dve.tensor_copy(kv_lat[:, 0:2, :], psum[:, 2:4, 0:KVL + PE2]).then_inc(lat_sb, 1)
            dve.tensor_copy(kv_lat[:, 2:4, :], psum[:, 4:6, 0:KVL + PE2]).then_inc(lat_sb, 1)
            dve.wait_ge(lat_sb, 3)
            dve.wait_ge(turn_full, FULL + 2)
            for i in range(6):
                v = q_lat[:, i, :] if i < 2 else kv_lat[:, i - 2, 0:KVL]
                n = v.shape[1]
                dve.tensor_tensor_reduce(out=xn_flat[:, 0:n], in0=v, in1=v, scale=1.0 / n, scalar=EPS, op0=ALU.mult, op1=ALU.add,
                                         accum_out=lat[:, 1, i:i + 1]).then_inc(lat_sq, 1)
                dve.wait_ge(lat_sq, i + 1)
            dve.wait_ge(lat_root, 1)
            dve.reciprocal(lat[:, 3, :], lat[:, 2, :]).then_inc(lat_sq, 1)
            dve.wait_ge(lat_sq, 7)
            for i in range(6):
                v = q_lat[:, i, :] if i < 2 else kv_lat[:, i - 2, 0:KVL]
                dve.tensor_scalar(v, v, lat[:, 3, i:i + 1], None, ALU.mult).then_inc(lat_n, 1)

            def xm_half(i, first):
                for c in range(4):
                    dve.wait_ge(xt_full, 4 * i + c + 1)
                    dve.tensor_copy(xm[:, 4 * i + c, :, 2:2 + T], psum[:, first[c], :].rearrange("p (s t) -> p s t", s=2))\
                       .then_inc(xt_sb, 1)

            def rotate(src, cos, sin, a, b, half, done, n0):
                dve.tensor_tensor(a, src, cos, ALU.mult).then_inc(done, 1)
                bv, sv, cv = [half(v) for v in (b, src, sin)]
                for k in range(2):
                    dve.tensor_tensor(bv[k], sv[1 - k], cv[k], ALU.mult).then_inc(done, 1)
                dve.wait_ge(done, n0 + 3)

            xm_half(0, (4, 5, 6, 7))
            cos2 = const("cos2").rearrange("p (t d) -> p t d", t=TT)
            sin2 = const("sin2").rearrange("p (t d) -> p t d", t=TT)

            def halves(v):
                r = v.rearrange("p a (h k d) -> p a h k d", h=2, k=2)
                return [r[:, :, :, k, :] for k in range(2)]

            key = kv_lat[:, 2:4, KVL:KVL + PE2]
            ta = xn_flat[:, 0:128].rearrange("p (t d) -> p t d", t=TT)
            tb = xn_flat[:, 128:256].rearrange("p (t d) -> p t d", t=TT)
            rotate(key, cos2, sin2, ta, tb, halves, kpe_sb, 0)
            xm_half(1, (6, 7, 0, 1))
            dve.wait_ge(lt_full, 2)
            for k in range(2):
                dve.tensor_scalar(kvlT[:, k, :], psum[:, 6 + k, :], col2["kv_norm_2"][:, k:k + 1], None, ALU.mult).then_inc(kvl_sb, 1)
            for n in range(2):
                dve.wait_ge(sig_sb, 3 + n)
                v = zg[:, :, n * UN:(n + 1) * UN]
                dve.tensor_tensor(v, v, gate_tmp[:, n, :, :], ALU.mult).then_inc(zg_sb, 1)
            dve.wait_ge(zg_sb, 2)
            for k in range(2):
                d = slice(PE2 * k, PE2 * (k + 1))
                dve.tensor_tensor(k_pe[:, 2:4, d], ta, tb, ALU.add).then_inc(kpe_sb, 1)
                dve.tensor_copy(k_pe[:, 0:2, d], kv_lat[:, 0:2, KVL:KVL + PE2]).then_inc(kpe_sb, 1)

            for n, b in enumerate((2, 4, 6, 0)):
                dve.wait_ge(slots_free, unit_done(U_UQ + n))
                dve.tensor_copy(q_tok[:, :, 384 * n:384 * n + 384], psum[:, b:b + 2, 0:384]).then_inc(q_sb, 1)

            def kv_tile(n):
                b = (4, 0)[n % 2]
                dve.wait_ge(slots_free, unit_done(U_UKV + n))
                v = psum[:, b:b + 2, :].rearrange("p t (h d) -> p t h d", h=2)
                dve.tensor_copy(k_tok[:, 2:4, 2 * n:2 * n + 2, :], v[:, :, :, 0:NOPE]).then_inc(kv_v, 1)
                dve.tensor_copy(v_tok[:, 2:4, 2 * n:2 * n + 2, :], v[:, :, :, NOPE:NOPE + VD]).then_inc(kv_v, 1)

            kv_tile(0)
            dve.wait_ge(q_sb, 4)
            qa = xn_flat[:, 0:512].rearrange("p (h d) -> p h d", h=H2)
            qb = xn_flat[:, 512:1024].rearrange("p (h d) -> p h d", h=H2)
            dve.wait_ge(kpe_sb, 7)
            for t in range(TT):
                src = q_tok[:, t, :].rearrange("p (h d) -> p h d", h=H2)[:, :, NOPE:NOPE + PE2]
                dst = q_pe[:, t, :].rearrange("p (h d) -> p h d", h=H2)
                dve.tensor_tensor(qa, src, cos2[:, t, :].unsqueeze(1).to_broadcast([P, H2, PE2]), ALU.mult).then_inc(qpe_sb, 1)
                for half in range(2):
                    for k in range(2):
                        o, s = 32 * half + 16 * k, 32 * half + 16 * (1 - k)
                        ins = dve.tensor_tensor(qb[:, :, o:o + 16], src[:, :, s:s + 16],
                                                sin2[:, t, o:o + 16].unsqueeze(1).to_broadcast([P, H2, 16]), ALU.mult)
                        if half == 1 and k == 1:
                            ins.then_inc(qpe_sb, 1)
                dve.wait_ge(qpe_sb, 3 * t + 2)
                dve.tensor_tensor(dst, qa, qb, ALU.add).then_inc(qpe_sb, 1)
                dve.wait_ge(qpe_sb, 3 * t + 3)
            for n in range(1, 4):
                kv_tile(n)
            dve.wait_ge(qt_full, 2)
            dve.tensor_copy(hT[:, 4:8, :], flat[2].rearrange("p (h t) -> p h t", h=4)).then_inc(qt_v, 1)
            dve.wait_ge(qt_full, 4)
            dve.tensor_copy(kpT, psum[:, 0, :]).then_inc(qt_v, 1)
            for i, db in ((1, 2), (3, 0)):
                dve.wait_ge(qt_full, 5 + i)
                dve.tensor_copy(kT2[:, 2 * i:2 * i + 2, :], DB[db]).then_inc(qt_v, 1)

            taps, bias = col2["conv_w_2"], col2["conv_b_2"]
            conv = [0]

            def tap(c, i):
                src = xm[:, c, :, i:i + T]
                wt = taps[:, i * KC + c:i * KC + c + 1]
                if i == 0:
                    ins = dve.tensor_scalar(xc[:, c, :, :], src, wt, bias[:, c:c + 1], ALU.mult, ALU.add)
                else:
                    dve.wait_ge(conv_s, conv[0])
                    ins = dve.scalar_tensor_tensor(out=xc[:, c, :, :], in0=src, scalar=wt, in1=xc[:, c, :, :],
                                                   op0=ALU.mult, op1=ALU.add)
                ins.then_inc(conv_s, 1)
                conv[0] += 1

            NJ2 = H2 * TT
            dve.wait_ge(xt_sb, 8)
            dve.wait_ge(xm_pad, 2)
            for j in range(NJ2 + 2):
                if j < NJ2:
                    dve.wait_ge(s2_full, j + 1)
                    dve.tensor_reduce(mx2[:, j:j + 1], psum[:, j % 2, :], AX_X, ALU.max, negate=True).then_inc(s2_v, 1)
                    dve.wait_ge(s2_v, 2 * j + 1)
                    dve.tensor_scalar(nmx2[:, j:j + 1], mx2[:, j:j + 1], SCALE2, None, ALU.mult).then_inc(s2_v, 1)
                    c = j // 2
                    for i in ((0, 1, 2), (3, 4))[j % 2]:
                        tap(c, i)
                if j >= 2:
                    i = j - 2
                    h, t = i // TT, i % TT
                    dve.wait_ge(e2_sb, i + 1)
                    dve.reciprocal(rden2[:, i:i + 1], den2[:, i:i + 1]).then_inc(r2_v, 1)
                    dve.wait_ge(r2_v, i + 1)
                    dve.wait_ge(y2_full, i + 1)
                    v = gated[:, t, h * VD:(h + 1) * VD]
                    dve.wait_ge(sig_sb, 6)
                    dve.scalar_tensor_tensor(out=v, in0=psum[:, 4 + i % 2, 0:VD], scalar=rden2[:, i:i + 1], in1=v,
                                             op0=ALU.mult, op1=ALU.mult).then_inc(y2_sb, 1)

            for c in range(0, KC, 2):
                dve.wait_ge(qk2_full, c + 1)
                dve.tensor_copy(qkF[:, :, c, :], DB[c % 4]).then_inc(qk2_v, 1)
            for t in range(TT):
                dve.wait_ge(sk_full, t + 1)
                dve.tensor_tensor(skip_tmp[:, t, :], flat[t], zg[:, t, :], ALU.mult).then_inc(sk_v, 1)
                dve.wait_ge(sk_v, 2 * t + 1)
                dve.wait_ge(y2_sb, NJ2)
                dve.tensor_tensor(gated[:, t, :], gated[:, t, :], skip_tmp[:, t, :], ALU.add).then_inc(sk_v, 1)
            dve.wait_ge(sk_v, 4)
            dve.wait_ge(gp_full, 1)
            dve.wait_ge(gp_zero, 1)
            for j in range(4):
                dve.tensor_copy(gp[32 * j:32 * j + 16, :], psum[32 * j:32 * j + 16, 4, :]).then_inc(gp_sb, 1)

            def value_tile(t):
                dve.wait_ge(vt_full, t + 1)
                dve.tensor_copy(v_ml[:, t, :, 0:MD], flat[t % 2].rearrange("p (h d) -> p h d", h=MH)).then_inc(vt_sb, 1)

            value_tile(0)
            dve.wait_ge(gr_full, 1)
            dve.wait_ge(b_in, 64)
            n = [0]

            def step(ins):
                ins.then_inc(gr_v, 1)
                n[0] += 1
                dve.wait_ge(gr_v, n[0])

            step(dve.tensor_scalar(gi, psum[0:8, 6, :], b_if[0:8, 0:1], None, ALU.add))
            step(dve.tensor_scalar(Ff, psum[0:8, 7, :], b_if[0:8, 1:2], None, ALU.add))
            step(dve.scalar_tensor_tensor(out=Fb, in0=Ff, scalar=-1.0, in1=Ff, op0=ALU.mult, op1=ALU.max))
            dve.wait_ge(gr_a, 2)
            step(dve.scalar_tensor_tensor(out=lf, in0=Ff, scalar=0.0, in1=Fb, op0=ALU.min, op1=ALU.subtract))
            back = lambda v, a, b: v[:, a:b][:, ::-1]
            step(dve.tensor_tensor_scan(out=Ff, data0=lf, data1=lf, initial=0.0, op0=ALU.add, op1=ALU.min))
            step(dve.tensor_tensor_scan(out=back(Fb, 0, T), data0=back(lf, 0, T), data1=back(lf, 0, T), initial=0.0,
                                        op0=ALU.add, op1=ALU.min))
            step(dve.tensor_tensor_scan(out=back(Fb, T, 2 * T), data0=back(lf, T, 2 * T), data1=back(lf, T, 2 * T),
                                        initial=Fb[:, 0:1], op0=ALU.add, op1=ALU.min))
            step(dve.tensor_tensor(af, gi, Ff, ALU.subtract))
            step(dve.tensor_tensor(ab, gi, Fb, ALU.subtract))
            step(dve.tensor_tensor_scan(out=Gf, data0=af, data1=af, initial=0.0, op0=ALU.max, op1=ALU.max))
            step(dve.tensor_tensor_scan(out=back(Gb, 0, T), data0=back(ab, 0, T), data1=back(ab, 0, T), initial=0.0,
                                        op0=ALU.max, op1=ALU.max))
            step(dve.tensor_tensor_scan(out=back(Gb, T, 2 * T), data0=back(ab, T, 2 * T), data1=back(ab, T, 2 * T),
                                        initial=Gb[:, 0:1], op0=ALU.max, op1=ALU.max))
            step(dve.tensor_tensor(lf[:, 0:T], Ff[:, T:2 * T], Gf[:, T:2 * T], ALU.add))
            step(dve.tensor_tensor(lf[:, T:2 * T], Fb[:, T:2 * T], Gb[:, T:2 * T], ALU.add))
            for t in range(1, 4):
                value_tile(t)
            dve.wait_ge(at_full, 1)
            dve.tensor_copy(aT.rearrange("p d t r -> p (d t r)"), psum[:, 4, 0:64]).then_inc(at_sb, 1)
            dve.wait_ge(at_sb, 3)

            masks = [const("before"), const("after")]
            def mask_rows(h):
                dve.wait_ge(raw_full, 2 * h + 1)
                dve.wait_ge(vt_full, 4)
                if h:
                    dve.wait_ge(dec_a, 10 * h)
                for d in range(2):
                    g = psum[:, 2 + h % 2, d * T:(d + 1) * T].rearrange("p (t n) -> p t n", t=TT)
                    dve.tensor_tensor(masked[:, d, :, :], g, masks[d].unsqueeze(1).to_broadcast([P, TT, P]), ALU.add).then_inc(dec_v, 1)

            def weights(h):
                dve.wait_ge(raw_full, 2 * h + 2)
                dve.wait_ge(dec_a, 10 * h + 10)
                dec = [decays[h % 2][:, d, :, :].rearrange("p s t -> p (s t)") for d in range(2)]
                for d, a, b in ((0, 0, 768), (0, 896, 1024), (1, 0, 640), (1, 768, 1024)):
                    dve.scalar_tensor_tensor(out=dec[d][:, a:b], in0=flat[0][:, a:b], scalar=MD ** -0.5, in1=dec[d][:, a:b],
                                             op0=ALU.mult, op1=ALU.mult).then_inc(w_v, 1)

            mask_rows(0)
            weights(0)
            for h in range(MH):
                if h + 1 < MH:
                    mask_rows(h + 1)
                    weights(h + 1)
                dve.wait_ge(num_full, h + 1)
                hv = 8 * h
                dve.tensor_copy(dens[:, 0, :], psum[:, 4:8, MD]).then_inc(h_v, 1)
                dve.wait_ge(h_v, hv + 1)
                dve.scalar_tensor_tensor(out=dens[:, 1, :], in0=dens[:, 0, :], scalar=-1.0, in1=dens[:, 0, :],
                                         op0=ALU.mult, op1=ALU.max).then_inc(h_v, 1)
                dve.wait_ge(h_v, hv + 2)
                dve.tensor_tensor(dens[:, 2, :].rearrange("p (d t) -> p d t", d=2),
                                  dens[:, 1, :].rearrange("p (d t) -> p d t", d=2), em[:, :, :, h], ALU.max).then_inc(h_v, 1)
                dve.wait_ge(h_v, hv + 3)
                dve.reciprocal(dens[:, 3, :], dens[:, 2, :]).then_inc(h_v, 1)
                dve.wait_ge(h_v, hv + 4)
                for t in range(TT):
                    v = h_tok[:, t, h * MD:(h + 1) * MD]
                    dve.tensor_scalar(v, psum[:, 4 + t, 0:MD], dens[:, 3, t:t + 1], None, ALU.mult).then_inc(h_v, 1)
                    dve.wait_ge(h_v, hv + 5 + 2 * t)
                    dve.scalar_tensor_tensor(out=v, in0=psum[:, 6 + t, 0:MD], scalar=dens[:, 3, 2 + t:3 + t], in1=v,
                                             op0=ALU.mult, op1=ALU.add).then_inc(h_v, 1)
            dve.wait_ge(hn_a, 8)
            dve.tensor_scalar(hst[:, 1, :], hst[:, 0, :], 1.0 / MD, EPS, ALU.mult, ALU.add).then_inc(mix_v, 1)
            dve.wait_ge(hn_a, 9)
            dve.reciprocal(hst[:, 3, :], hst[:, 2, :]).then_inc(mix_v, 1)
            dve.wait_ge(mix_v, 2)
            dve.wait_ge(mlrow_in, 16)
            for h in range(MH):
                for t in range(TT):
                    v = h_tok[:, t, h * MD:(h + 1) * MD]
                    dve.scalar_tensor_tensor(out=v, in0=v, scalar=hst[:, 3, 2 * h + t:2 * h + t + 1],
                                             in1=ml_row[:, h * MD:(h + 1) * MD], op0=ALU.mult, op1=ALU.mult).then_inc(mix_v, 1)
            dve.wait_ge(mix_v, 10)
            dve.tensor_tensor(h_tok, h_tok, zg, ALU.mult).then_inc(mix_v, 1)
            dve.wait_ge(mix_v, 11)
            dve.tensor_tensor(gated, gated, h_tok, ALU.add).then_inc(mix_v, 1)
            dve.wait_ge(turn_full, FULL + 5)
            dve.tensor_copy(hT[:, 0:4, :], flat[2].rearrange("p (k t) -> p k t", k=4)).then_inc(turn_v, 1)

            def add_gated(first, ready):
                for n in range(2):
                    dve.wait_ge(*ready(n))
                    g = g_row[:, n * UN:(n + 1) * UN].unsqueeze(1).to_broadcast([P, TT, UN])
                    if n:
                        dve.wait_ge(x2_v, first + 2)
                    dve.tensor_tensor(x_tmp, DB[n], g, ALU.mult).then_inc(x2_v, 1)
                    dve.wait_ge(x2_v, first + 2 * n + 1)
                    v = x[:, :, n * UN:(n + 1) * UN]
                    dve.tensor_tensor(v, v, x_tmp, ALU.add).then_inc(x2_v, 1)
                dve.wait_ge(x2_v, first + 4)

            dve.wait_ge(gb_sb, 1)
            add_gated(0, lambda n: (slots_free, unit_done(U_OUT + 2 * n + 1)))
            norm(8, x, xn)
            turn_modulated(FULL + 7, hT, lambda k: amp2[:, k, :], lambda k: modT[:, 24 + k, 0:1])
            dve.wait_ge(lg_full, 1)
            dve.tensor_reduce(rst[:, 0, :], psum[:, 0, 0:TT * NE].rearrange("p (t e) -> p t e", t=TT), AX_X, ALU.max, negate=True)\
               .then_inc(rt_v, 1)
            dve.wait_ge(rt_a, 2)
            dve.reciprocal(rst[:, 2, :], rst[:, 1, :]).then_inc(rt_v, 1)
            dve.wait_ge(rt_v, 2)
            for t in range(TT):
                dve.tensor_scalar(aff[:, t, :], aff[:, t, :], rst[:, 2, t:t + 1], None, ALU.mult).then_inc(rt_v, 1)
            n[0] = 0

            def top_step(ins):
                ins.then_inc(top_v, 1)
                n[0] += 1
                dve.wait_ge(top_v, n[0])

            dve.wait_ge(af_full, 1)
            top_step(dve.tensor_copy(affT, psum[0:NE, 1, 0:T]))
            for r in range(CAP // 8):
                eight = slice(8 * r, 8 * r + 8)
                top_step(dve.max(top[:, eight], affT))
                top_step(dve.max_index(topi[:, eight], top[:, eight], affT))
                top_step(dve.match_replace(affT, top[:, eight], affT, -1.0))
            top_step(dve.tensor_copy(topf, topi))
            for i, v in enumerate((topf, top)):
                top_step(dve.tensor_tensor(wide[0:NE, i, :, :], v.unsqueeze(1).to_broadcast([NE, NE, CAP]),
                                           ident[0:NE, 0:NE].unsqueeze(2).to_broadcast([NE, NE, CAP]), ALU.mult))
            dve.wait_ge(sl_full, 1)
            dve.tensor_copy(slotT.rearrange("p a b c -> p (a b c)"), psum[:, 5, 0:8]).then_inc(sl_v, 1)
            for t in range(TT):
                dve.tensor_scalar(pick[:, t, :], psum[:, 4, :], const("token")[:, t:t + 1], None, ALU.is_equal).then_inc(sl_v, 1)
            dve.wait_ge(sl_v, 1)
            for g in range(4):
                dve.tensor_scalar(pickT[:, g, :], const("iota"), slotT[:, 0, g, :], slotT[:, 1, g, :], ALU.is_equal, ALU.mult)\
                   .then_inc(sl_v, 1)
            for c in range(0, KC, 2):
                dve.wait_ge(xs_full, c + 1)
                dve.tensor_scalar(xsT[:, c, :], psum[:, c, :], amp2[:, c, :], modT[:, 24 + c, 0:1], ALU.mult, ALU.add).then_inc(xs_v, 1)
            dve.sem_inc(ye_sb, 1)
            with dve.Fori(0, NE // EG) as g:
                for n_ in range(2):
                    dve.wait_ge(slots_free, g * 48 + unit_done(U_EX + 8 * (2 + n_) + 7))
                    dve.wait_ge(hid_a, g * 2 + n_ + 1)
                    dve.tensor_tensor(hid_u[:, n_ * UN:(n_ + 1) * UN], psum[:, 2 + n_, :], hid[:, n_, :], ALU.mult).then_inc(hid_v, 1)
                for n_ in range(2):
                    dve.wait_ge(slots_free, g * 48 + unit_done(U_EX + 8 * (4 + n_) + 7))
                    dve.tensor_copy(y_ex[:, g, n_ * UN:(n_ + 1) * UN], psum[:, 6 + n_, :]).then_inc(ye_sb, 1)
            dve.wait_ge(gb_sb, 2)
            add_gated(4, lambda n: (sc_full, n + 1))
            norm(9, x, xn)
            dve.wait_ge(fin_row_in, 16)
            dve.wait_ge(norm_v, 50)
            for t in range(TT):
                dve.tensor_tensor(xn[:, t, :], xn[:, t, :], last_row, ALU.mult).then_inc(fin_v, 1)

        def scalar_block2(act, norm):
            act.wait_ge(dn_x, 2 * DEPTH)
            act.wait_ge(turn_full, FULL)
            norm(5, x, xn)
            act.wait_ge(x_row, 1)
            norm(6, x, xn)
            act.wait_ge(ctx_in, 16)
            norm(7, ctx_x, ctx_n)
            def high_parts(first, last):
                for i in range(first, last + 1):
                    split2_hi(act, i)

            high_parts(0, 3)
            act.wait_ge(mod_sb, 5)

            def turn_modulated(full, dst, amp, shift):
                act.wait_ge(turn_full, full)
                for k in range(4):
                    act.activation(dst[:, 4 + k, :], flat[3][:, k * T:(k + 1) * T], ACT.Identity, scale=amp(4 + k), bias=shift(4 + k))\
                       .then_inc(turn_a, 1)

            for i, m in enumerate((0, 1)):
                turn_modulated(FULL + 2 + 2 * i, hT2[:, :, T * (1 - m):T * (2 - m)],
                               lambda k: amp1[:, k, m:m + 1], lambda k: modT[:, k, m:m + 1])

            def xm_half(i):
                for k, b in enumerate(((6, 0), (0, 2))[i]):
                    act.wait_ge(slots_free, unit_done(U_IN + (5, 9)[i]))
                    if i:
                        act.wait_ge(xt_full, 4)
                    act.activation(xm_tok[:, 2 * k:2 * k + 2, :], psum[:, b:b + 2, :], ACT.Copy).then_inc(xm_sb, 1)

            def sigmoid(i, dst, b):
                act.wait_ge(slots_free, unit_done(U_IN + 2 * i + 1))
                act.activation(dst, psum[:, b:b + 2, :], ACT.Sigmoid).then_inc(sig_sb, 1)

            high_parts(4, 8)
            xm_half(0)
            act.wait_ge(lat_sq, 6)
            act.activation(lat[:, 2, :], lat[:, 1, :], ACT.Sqrt).then_inc(lat_root, 1)
            high_parts(9, 10)
            sigmoid(3, zg[:, :, 0:UN], 2)
            high_parts(11, 12)
            xm_half(1)
            high_parts(13, 14)
            sigmoid(5, zg[:, :, UN:D], 4)
            high_parts(15, 16)
            sigmoid(6, gate_tmp[:, 0, :, :], 2)
            act.wait_ge(lt_full, 1)
            for k in range(3):
                act.activation(qlT[:, k, :], flat[2][:, k * T:(k + 1) * T], ACT.Copy, scale=col2["q_norm_2"][:, k:k + 1])\
                   .then_inc(ql_sb, 1)
            high_parts(17, 18)
            sigmoid(7, gate_tmp[:, 1, :, :], 0)
            high_parts(19, 19)
            sigmoid(8, gated[:, :, 0:UN], 2)
            sigmoid(9, gated[:, :, UN:D], 0)
            for n in range(4):
                b = (2, 6)[n % 2]
                act.wait_ge(slots_free, unit_done(U_UKV + n))
                v = psum[:, b:b + 2, :].rearrange("p t (h d) -> p t h d", h=2)
                act.activation(k_tok[:, 0:2, 2 * n:2 * n + 2, :], v[:, :, :, 0:NOPE], ACT.Copy).then_inc(kv_a, 1)
                act.activation(v_tok[:, 0:2, 2 * n:2 * n + 2, :], v[:, :, :, NOPE:NOPE + VD], ACT.Copy).then_inc(kv_a, 1)
            act.wait_ge(qt_full, 1)
            act.activation(hT[:, 0:4, :], flat[1].rearrange("p (h t) -> p h t", h=4), ACT.Copy).then_inc(qt_a, 1)
            act.wait_ge(qt_full, 3)
            act.activation(qpT, flat[3].rearrange("p (h t) -> p h t", h=4), ACT.Copy).then_inc(qt_a, 1)
            for i, db in ((0, 1), (2, 3)):
                act.wait_ge(qt_full, 5 + i)
                act.activation(kT2[:, 2 * i:2 * i + 2, :], DB[db], ACT.Copy).then_inc(qt_a, 1)

            NJ2 = H2 * TT
            for j in range(NJ2 + 1):
                if j < NJ2:
                    act.wait_ge(s2_v, 2 * j + 2)
                    if j >= 2:
                        act.wait_ge(t2_full, j - 1)
                    act.activation(prob[:, j % 2, :], psum[:, j % 2, :], ACT.Exp, scale=SCALE2, bias=nmx2[:, j:j + 1],
                                   accum_out=den2[:, j:j + 1]).then_inc(e2_sb, 1)
                if j >= 1:
                    i = j - 1
                    act.wait_ge(t2_full, i + 1)
                    if i >= 2:
                        act.wait_ge(y2_full, i - 1)
                    act.activation(probT[:, i % 2, :, :], psum[:, 2 + i % 2, :].rearrange("p (b q) -> p b q", b=4), ACT.Copy)\
                       .then_inc(t2_sb, 1)
            for i in range(4):
                act.wait_ge(conv_s, 10 * i + 10)
                v = xc[:, 2 * i:2 * i + 2, :, :].rearrange("p c s t -> p (c s t)")
                act.activation(v, v, ACT.Silu).then_inc(xc_sb, 1)
            for c in range(1, KC, 2):
                act.wait_ge(qk2_full, c + 1)
                act.activation(qkF[:, :, c, :], DB[c % 4], ACT.Copy).then_inc(qk2_a, 1)
            act.wait_ge(qk2_full, KC)
            act.wait_ge(skip_sb, 2)
            for i in range(4):
                act.wait_ge(vf_full, i + 1)
                act.activation(vF[:, 2 * i:2 * i + 2, :], DB[2 + i % 2], ACT.Copy).then_inc(vf_sb, 1)
            act.wait_ge(gr_v, 3)
            act.activation(Fb, Fb, ACT.Exp, scale=-1.0).then_inc(gr_a, 1)
            act.wait_ge(gr_a, 1)
            act.activation(Fb, Fb, ACT.Ln, bias=1.0).then_inc(gr_a, 1)
            act.wait_ge(at_full, 1)
            act.wait_ge(at_sb, 1)
            for d in range(2):
                c0 = 64 + 16 * d
                v = psum[:, 4, c0:c0 + 16].rearrange("p (t r) -> p t r", t=TT)[:, :, 4 * d:4 * d + 4]
                act.activation(em[:, d, :, :], v, ACT.Exp, scale=-1.0).then_inc(at_sb, 1)
            act.wait_ge(at_sb, 3)
            for h in range(MH):
                act.wait_ge(dec_v, 2 * h + 2)
                decay = decays[h % 2]
                if h >= 2:
                    act.wait_ge(num_full, h - 1)
                act.wait_ge(gp_full, 1)
                for d in range(2):
                    g = psum[:, 2 + h % 2, d * T:(d + 1) * T]
                    r = 4 * d + h
                    whole, part = (slice(P, 2 * P), 2) if d == 0 else (slice(0, P), 3)
                    todo = [(0, slice(0, T), g), (1, slice(0, T), g),
                            (2, slice(0, P), masked[:, d, 0, :]), (3, slice(P, 2 * P), masked[:, d, 1, :]),
                            (part, whole, g[:, whole])]
                    for s, cols_, src in todo:
                        act.activation(decay[:, d, s, cols_], src, ACT.Exp, scale=-1.0, bias=aT[:, d, s, r:r + 1]).then_inc(dec_a, 1)
                if h:
                    squares_of(act, h - 1)
            squares_of(act, MH - 1)
            act.wait_ge(mix_v, 1)
            act.activation(hst[:, 2, :], hst[:, 1, :], ACT.Sqrt).then_inc(hn_a, 1)
            act.wait_ge(gb_full, 1)
            act.activation(g_row, flat[1], ACT.Copy).then_inc(gb_sb, 1)
            act.wait_ge(turn_full, FULL + 6)
            act.activation(hT[:, 4:8, :], flat[3].rearrange("p (k t) -> p k t", k=4), ACT.Copy).then_inc(turn_a, 1)
            act.wait_ge(x2_v, 4)
            norm(8, x, xn)
            turn_modulated(FULL + 8, hT, lambda k: amp2[:, k, :], lambda k: modT[:, 24 + k, 0:1])
            act.wait_ge(rt_v, 1)
            for t in range(TT):
                act.activation(aff[:, t, :], psum[:, 0, t * NE:(t + 1) * NE], ACT.Exp, bias=rst[:, 0, t:t + 1],
                               accum_out=rst[:, 1, t:t + 1]).then_inc(rt_a, 1)
            act.wait_ge(gb_full, 2)
            act.activation(g_row, flat[1], ACT.Copy).then_inc(gb_sb, 1)
            for c in range(1, KC, 2):
                act.wait_ge(xs_full, c + 1)
                act.activation(xsT[:, c, :], psum[:, c, :], ACT.Identity, scale=amp2[:, c, :], bias=modT[:, 24 + c, 0:1]).then_inc(xs_a, 1)
            with act.Fori(0, NE // EG) as g:
                for n in range(2):
                    act.wait_ge(slots_free, g * 48 + unit_done(U_EX + 8 * n + 7))
                    act.activation(hid[:, n, :], psum[:, n, :], ACT.Silu).then_inc(hid_a, 1)
                act.wait_ge(ht_full, g + 1)
                act.activation(hidT.rearrange("p k n -> p (k n)"), flat[2], ACT.Copy).then_inc(ht_sb, 1)
            act.wait_ge(x2_v, 8)
            norm(9, x, xn)

        def squares_of(act, h):
            act.wait_ge(h_v, 8 * h + 8)
            for t in range(TT):
                i = 2 * h + t
                if i:
                    act.wait_ge(hn_a, i)
                act.activation(junk, h_tok[:, t, h * MD:(h + 1) * MD], ACT.Square, accum_out=hst[:, 0, i:i + 1]).then_inc(hn_a, 1)

        def gpsimd_block2(pool):
            pool.wait_ge(s_v, 2 * NJ * DEPTH)
            pool.wait_ge(mem_g, 2 * DEPTH)
            pool.wait_ge(slots_free, (DEPTH - 1) * UNITS1 + unit_done(47))
            pool.dma_start(ctx_x, w["ctx_2"].rearrange("b (t p) d -> p (b t) d", p=P)).then_inc(ctx_in, 16)
            pool.wait_ge(slots_free, unit_done(U_IN - 1))
            for side in (0, 2 + T):
                pool.memset(xm[:, :, :, side:side + 2], 0.0).then_inc(xm_pad, 1)
            for i, name in enumerate(("w_qblk_2", "w_kblk_2", "w_vblk_2")):
                pool.dma_start(blk[:, i, :, :], w[name][0].rearrange("(c n) j k -> (n j) c k", c=KC)).then_inc(blk_in, 16)
            for d in range(2):
                for kind in range(2):
                    c0 = 8 * d + 4 * kind
                    pool.dma_start(b_if[4 * d:4 * d + 4, kind:kind + 1], w["b_gate_2"][0, c0:c0 + 4].rearrange("(h o) -> h o", o=1))\
                        .then_inc(b_in, 16)
            for i in range(2 * len(IN_TILES)):
                split2_lo(pool, i)
            pool.wait_ge(slots_free, unit_done(U_UKV + 3))
            pool.dma_start(wg, w["w_gate_2"][0].rearrange("(c p) g -> p c g", p=P)).then_inc(wg_in, 16)
            pool.wait_ge(blk_in, 48)
            pool.wait_ge(qpe_sb, 6)
            where = const("block4")
            for i in range(3):
                for half in range(2):
                    cs = slice(4 * half, 4 * half + 4)
                    o = bd[i][:, cs, :].rearrange("p c (n k) -> p c n k", k=4)
                    a = blk[:, i, cs, :].unsqueeze(2).to_broadcast([P, 4, 32, 4])
                    b = where.unsqueeze(1).unsqueeze(3).to_broadcast([P, 4, 32, 4])
                    ins = pool.tensor_tensor(o, a, b, ALU.mult)
                ins.then_inc(bd_sb, 1)
            pool.wait_ge(s2_full, H2 * TT)
            for half in range(2):
                cs = slice(4 * half, 4 * half + 4)
                pool.wait_ge(xc_sb, 2 * half + 2)
                pool.tensor_tensor(skipped[:, cs, :], xc[:, cs, 1, :], col2["ml_skip_2"][:, cs].unsqueeze(2).to_broadcast([P, 4, T]),
                                   ALU.mult).then_inc(skip_sb, 1)
            pool.wait_ge(sk_full, 2)
            pool.memset(gp, 0.0).then_inc(gp_zero, 1)
            pool.wait_ge(sk_v, 4)
            pool.memset(v_ml[:, :, :, MD:MD + 1], 1.0).then_inc(ones_sb, 1)
            pool.wait_ge(vt_full, 4)
            pool.dma_start(ml_row, w["ml_norm_2"][0].partition_broadcast(P)).then_inc(mlrow_in, 16)
            pool.wait_ge(mt_full, 3)
            pool.dma_start(wr, w["w_router_2"][0].rearrange("(c p) e -> p c e", p=P)).then_inc(wr_in, 16)
            pool.wait_ge(num_full, MH)
            pool.dma_start(last_row, w["final_norm_2"].partition_broadcast(P)).then_inc(fin_row_in, 16)
            pool.wait_ge(xs_v, 4)
            pool.wait_ge(xs_a, 4)
            with pool.Fori(0, NE // EG) as g:
                pool.wait_ge(slots_free, g * 48 + unit_done(U_EX - 17))
                pool.tensor_copy(stage, xsT[:, :, bass.ts(g, P)]).then_inc(stage_sb, 1)

        @block.sync
        def _(sp):
            sp.sem_inc(slots_free, R1)
            sp.dma_start(x[:, :, :], w["mem"].rearrange("b (t p) d -> p (b t) d", p=P)).then_inc(mem_in, 16)
            sp.dma_start(consts[:, :], w["consts"]).then_inc(const_in, 16)
            for i, g in enumerate(("norm_mix", "norm_mem", "norm_mlp")):
                sp.dma_start(rows1[16 * i:16 * i + 16, :], w[g].rearrange("l (c p) -> (l c) p", p=P)).then_inc(const_in, 16)
            for name, a, n in ROWS2:
                sp.dma_start(rows2[a:a + n, :], rows_of(w[name])).then_inc(const_in, 16)
            sp.wait_ge(norm_v, 5)
            sp.dma_start(x[:, :, :], w["x"].rearrange("b (t p) d -> p (b t) d", p=P)).then_inc(x_in, 16)

            def load(u, src, done, seen=False):
                sp.wait_ge(slots_free, done)
                if seen:
                    sp.sem_inc(s_seen, 1)
                c, n = src.shape[1], src.shape[2]
                dst = slot(u)[:, 0:c, 0:n]
                sp.dma_start(dst, src).then_inc(landed(u), 16)

            with sp.Fori(0, DEPTH) as l:
                for u, src in enumerate(layer_units(l)):
                    load(u, src, l * UNITS1 + u + 1)
                    if u in (52, 53, 56, 57, 60, 61):
                        q, j0 = (u - 52) // 4, 2 * (u % 4)
                        if q and j0 == 0:
                            sp.wait_ge(mod_full, l * 3 + q)
                        for j in (j0, j0 + 1):
                            c0 = UN * (4 * q + j)
                            sp.dma_start(mod_slot[j], w["w_mod_2"][0].rearrange("(h c p) n -> h p c n", h=DEPTH, p=P)[l, :, :, c0:c0 + UN])\
                              .then_inc(mod_in, 16)
            sync_block2(sp, load)

        @block.tensor
        def _(pe):
            def unit_ready(u, l=0):
                if u >= U_EX:
                    s, rounds = ring_slot(u), l * (48 // RE) + (u - U_EX) // RE + 1
                    before = (U8 // R1 + 2 if s < R1 else 1) if s < R else 0
                    pe.wait_ge(landed(u), rounds * (16 if s < R else 64) + 16 * before)
                elif u >= U8:
                    before = U8 // R1 if ring_slot(u) < R1 else 0
                    pe.wait_ge(slot_in[ring_slot(u)], 16 * (before + (u - U8) // R + 1))
                elif u >= U_IN:
                    pe.wait_ge(lo_p, DEPTH * len(LO_POOL) + u - U_IN + 1)
                elif u in LO_VECTOR:
                    pe.wait_ge(lo_v, l * len(LO_VECTOR) + LO_VECTOR.index(u) + 1)
                elif u in LO_POOL:
                    pe.wait_ge(lo_p, l * len(LO_POOL) + LO_POOL.index(u) + 1)
                else:
                    pe.wait_ge(slot_in[u % R1], l * (UNITS1 // R1) * 16 + 16 * (u // R1 + 1))

            def product(dst, lhsT, k0, u, nk=UC, n=UN, start=True, stop=True, first=0):
                for k in range(nk):
                    last = pe.matmul(dst, lhsT(k0 + k), slot(u)[:, first + k, 0:n],
                                     start=start and k == 0, stop=stop and k == nk - 1)
                return last

            def split_product(dst, hi, lo, k0, u, nk=UC, start=True, stop=True, first=0, n=UN):
                for k in range(nk):
                    w_hi, w_lo = slot_hi(u)[:, first + k, 0:n], slot_lo(u)[:, first + k, 0:n]
                    pe.matmul(dst, lo(k0 + k), w_hi, start=start and k == 0, stop=False)
                    pe.matmul(dst, hi(k0 + k), w_lo, start=False, stop=False)
                    last = pe.matmul(dst, hi(k0 + k), w_hi, start=False, stop=stop and k == nk - 1)
                return last

            def split_tile(db, a, a_lo, u, l):
                for kh in range(2):
                    unit_ready(u + kh, l)
                    for t in range(TT):
                        last = split_product(db[:, t, :], tokens(a, t), tokens(a_lo, t), UC * kh, u + kh,
                                             start=kh == 0, stop=kh == 1)
                    last.then_inc(slots_free, 1)

            def tokens(a, t):
                return lambda k: a[:, k, t * P:(t + 1) * P]

            def tile_of(db, a, u, turns):
                for kh in range(2):
                    unit_ready(u + kh, turns)
                    for t in range(TT):
                        last = product(db[:, t, :], tokens(a, t), UC * kh, u + kh, start=kh == 0, stop=kh == 1)
                    last.then_inc(slots_free, 1)

            def to_features(src):
                for half in range(2):
                    for k in range(4):
                        for t in range(TT):
                            last = pe.transpose(flat[2 + half][:, k * T + t * P:k * T + (t + 1) * P],
                                                src[:, t, (4 * half + k) * P:(4 * half + k + 1) * P], ident)
                    last.then_inc(turn_full, 1)

            pe.wait_ge(const_in, 16 * N_CONST)
            pe.transpose(flat[0][:, 0:48], rows1[:, :], ident[0:48, 0:48])
            pe.transpose(flat[0][:, 48:48 + N_ROWS2], rows2[:, :], ident[0:N_ROWS2, 0:N_ROWS2]).then_inc(cols_full, 1)
            pe.wait_ge(norm_v, 5)
            to_features(xn)

            with pe.Fori(0, DEPTH) as l:
                pe.wait_ge(mem_g, l * 2 + 2)
                pe.wait_ge(x_ready, l + 1)
                tile_of(DB[0], memT, 0, l)
                pe.wait_ge(norm_v, l * 10 + 10)
                pe.wait_ge(turn_v, l * 9 + 1)
                pe.wait_ge(turn_a, l * 9 + 1)
                pe.wait_ge(mod_add, l * 3 + 1)
                to_features(xn)
                pe.wait_ge(kv_sb, l + 1)
                for c in range(2):
                    for t in range(TT):
                        last = pe.transpose(flat[1][:, c * T + t * P:c * T + (t + 1) * P],
                                            kv_mem[:, t, c * P:(c + 1) * P], ident)
                last.then_inc(km_full, 1)
                pe.wait_ge(turn_v, l * 9 + 5)
                pe.wait_ge(turn_a, l * 9 + 5)
                pe.wait_ge(turn_lo, l * 18 + 8)
                for n in range(5):
                    if n == 1:
                        pe.wait_ge(km_sb, l + 1)
                    if n >= 2:
                        pe.wait_ge(z_sb, l * 5 + n - 1)
                    split_tile(DB[n % 2], hT_hi, hT_lo, 2 + 2 * n, l)
                pe.wait_ge(rope_s, l * 8 + 8)
                pe.wait_ge(z_sb, l * 5 + 5)
                for b in range(4):
                    if b >= 2:
                        pe.wait_ge(qk_sb, l * 4 + b - 1)
                    for i in range(4 if b < 3 else 2):
                        for t in range(TT):
                            c0 = z_column(4 * b + i)
                            last = pe.transpose(flat[2 + b % 2][:, i * T + t * P:i * T + (t + 1) * P],
                                                z[:, t, c0:c0 + P], ident)
                    last.then_inc(qk_full, 1)
                pe.wait_ge(qk_sb, l * 4 + 4)
                for j in range(NJ + 1):
                    if j < NJ:
                        if j >= 2:
                            pe.wait_ge(s_v, l * (2 * NJ) + 2 * (j - 2) + 1)
                        job = JOBS[j]
                        q = slice(job["t"] * P, (job["t"] + 1) * P)
                        rows = slice(job["base"], job["base"] + HD)
                        col, i, bl = 0, 0, job["blocks"]
                        while i < len(bl):
                            qc, kc, kt, _ = bl[i]
                            wide = 2 if i + 1 < len(bl) and bl[i + 1][1] == kc else 1
                            keys = kmT if job["kind"] == "memory" else qkT
                            last = pe.matmul(flat[j % 2][:, col:col + wide * P], qkT[rows, qc, q],
                                             keys[rows, kc, kt * P:(kt + wide) * P], start=True, stop=True)
                            col += wide * P
                            i += wide
                        last.then_inc(s_full, 1)
                    if j >= 1:
                        pe.wait_ge(p_v, l * (2 * NJ) + 2 * j)
                        if j >= 2:
                            pe.wait_ge(o_sb, l * NJ + j - 1)
                        for i in range(len(JOBS[j - 1]["blocks"])):
                            last = pe.transpose(flat[2][:, i * P:(i + 1) * P], S[:, (j - 1) % 3, i * P:(i + 1) * P], ident)
                        last.then_inc(t_full, 1)

                    def gate_part(half):
                        g, kh, t = j // 4, (j // 2) % 2, j % 2
                        u = 12 + j // 2
                        if half == 0:
                            if t == 0:
                                unit_ready(u, l)
                            if j % 4 == 0 and g:
                                pe.wait_ge(g_exp, l * 6 + g)
                        last = split_product(DB[3][:, t, :], tokens(hT_hi, t), tokens(hT_lo, t), UC * kh + 2 * half, u, nk=2,
                                             first=2 * half, start=kh == 0 and half == 0, stop=kh == 1 and half == 1)
                        if half == 1 and t == 1:
                            last.then_inc(slots_free, 1)

                    if j < NJ:
                        gate_part(0)
                    if j >= 1:
                        job = JOBS[j - 1]
                        pe.wait_ge(t_sb, l * NJ + j)
                        for i, (_, _, kt, (src, c0)) in enumerate(job["blocks"]):
                            v = (z if src == "z" else kv_mem)[:, kt, c0:c0 + HD]
                            last = pe.matmul(flat[2][job["base"]:job["base"] + HD, 768:768 + P], v, PT[:, (j - 1) % 2, i, :],
                                             start=i == 0, stop=i == len(job["blocks"]) - 1)
                        last.then_inc(o_full, 1)
                    if j < NJ:
                        gate_part(1)
                pe.wait_ge(o_sb, (l + 1) * NJ)
                for n in range(2):
                    for b, (c0, nk) in enumerate(((0, 1), (1, 3), (4, 2))):
                        i, u = 3 * n + b, 24 + 2 * n + (b == 2)
                        if b != 1:
                            unit_ready(u, l)
                        if i >= 2:
                            pe.wait_ge(pj_sb, l * 6 + i - 1)
                        for t in range(TT):
                            last = product(DB[i % 2][:, t, :], tokens(oT, t), c0, u, nk=nk, first=c0 % 4)
                        last.then_inc(pa_full if b == 0 else slots_free, 1)
                pe.wait_ge(y_sum, l * 4 + 4)
                pe.wait_ge(g_exp, l * 6 + 6)
                to_features(xn)
                pe.wait_ge(turn_v, l * 9 + 6)
                pe.wait_ge(turn_a, l * 9 + 6)
                pe.wait_ge(turn_lo, l * 18 + 10)
                pe.wait_ge(pj_sb, l * 6 + 6)
                for n in range(2):
                    split_tile(DB[n], hT_hi, hT_lo, 28 + 2 * n, l)
                pe.wait_ge(norm_v, l * 10 + 15)
                to_features(xn)
                pe.wait_ge(turn_v, l * 9 + 10)
                pe.wait_ge(turn_a, l * 9 + 10)
                pe.wait_ge(turn_lo, l * 18 + 18)

                def squares(n):
                    pe.wait_ge(up_sb, l * 8 + n + 1)
                    if n >= 2:
                        pe.wait_ge(u_lo, l * 8 + n - 1)
                    for k in range(4):
                        for t in range(TT):
                            last = pe.transpose(flat[2 + n % 2][:, k * T + t * P:k * T + (t + 1) * P],
                                                r_up[:, n % 2, t, k * P:(k + 1) * P], ident)
                    last.then_inc(u_full, 1)

                for n in range(8):
                    if n >= 2:
                        pe.wait_ge(up_sb, l * 8 + n - 1)
                    split_tile(DB[n % 2], hT_hi, hT_lo, 32 + 2 * n, l)
                    if n:
                        squares(n - 1)
                squares(7)
                for kg in range(8):
                    pe.wait_ge(u_lo, l * 8 + kg + 1)
                    for n in range(2):
                        u = 48 + 2 * kg + n
                        unit_ready(u, l)
                        for t in range(TT):
                            last = split_product(DB[n][:, t, :], tokens(uT_hi, t), tokens(uT_lo, t), UC * kg, u,
                                                 start=kg == 0, stop=kg == 7)
                        last.then_inc(slots_free, 1)
                        if u in (52, 56, 62):
                            q = (52, 56, 62).index(u)
                            if q == 0:
                                pe.wait_ge(silu_l, l + 1)
                                pe.wait_ge(u_lo, l * 8 + 8)
                            pe.wait_ge(mod_in, l * 192 + 64 * (q + 1))
                            for k in range(UC):
                                for j in range(4):
                                    last = pe.matmul(psum[32 * j:32 * j + 32, 4 + q, :], silu_now[:, k, :], mod_slot[j][:, k, :],
                                                     start=k == 0, stop=k == UC - 1)
                            last.then_inc(mod_full, 1)
            tensor_block2(pe, unit_ready, product, tokens, tile_of, to_features, split_product)

        @block.vector
        def _(dve):
            def norm(call, src, dst):
                v = call * 5
                dve.tensor_tensor_reduce(out=dst[:, 1, :], in0=src[:, 1, :], in1=src[:, 1, :], scale=1.0, scalar=0.0,
                                         op0=ALU.mult, op1=ALU.add, accum_out=stat[:, 1, 0:1]).then_inc(norm_v, 1)
                dve.wait_ge(norm_v, v + 1)
                dve.wait_ge(norm_a, call * 2 + 1)
                dve.tensor_scalar(stat[:, :, 1:2], stat[:, :, 0:1], 1.0 / src.shape[2], EPS, ALU.mult, ALU.add)\
                   .then_inc(norm_v, 1)
                dve.wait_ge(norm_a, call * 2 + 2)
                dve.reciprocal(stat[:, :, 3:4], stat[:, :, 2:3]).then_inc(norm_v, 1)
                dve.wait_ge(norm_v, v + 3)
                for t in range(TT):
                    dve.tensor_scalar(dst[:, t, :], src[:, t, :], stat[:, t, 3:4], None, ALU.mult).then_inc(norm_v, 1)

            def turn_gain(call_full, gain, v, a):
                dve.wait_ge(turn_full, call_full)
                for k in range(4):
                    dve.tensor_scalar(hT_hi[:, k, :], flat[2][:, k * T:(k + 1) * T], gain[:, k:k + 1], None, ALU.mult)\
                       .then_inc(turn_v, 1)
                for k in range(KC):
                    if k == 0:
                        dve.wait_ge(turn_v, v)
                    if k == 4:
                        dve.wait_ge(turn_a, a)
                    dve.scalar_tensor_tensor(out=hT_lo[:, k, :], in0=flat[2 + k // 4][:, k % 4 * T:(k % 4 + 1) * T],
                                             scalar=gain[:, k:k + 1], in1=hT_hi[:, k, :].bitcast(F32), op0=ALU.mult, op1=ALU.subtract)\
                       .then_inc(turn_lo, 1)

            dve.wait_ge(mem_in, 16)
            norm(0, x, xn)
            dve.wait_ge(cols_full, 1)
            dve.tensor_copy(cols[:, :], flat[0][:, 0:48 + N_ROWS2]).then_inc(cols_sb, 1)
            dve.wait_ge(turn_full, 1)
            dve.tensor_copy(memnT[:, 0:4, :], flat[2].rearrange("p (k t) -> p k t", k=4)).then_inc(turn_v, 1)
            dve.wait_ge(turn_full, 2)
            dve.wait_ge(x_in, 16)
            dve.sem_inc(x_ready, 1)
            dve.sem_inc(mod_add, 1)

            with dve.Fori(0, DEPTH) as l:
                norm(l * 2 + 1, x, xn)
                dve.wait_ge(gains, l + 1)
                turn_gain(l * 6 + 3, g_now[:, 0, :], l * 9 + 5, l * 9 + 5)
                dve.wait_ge(slots_free, l * UNITS1 + unit_done(1))
                dve.tensor_copy(kv_mem[:, :, :], DB[0][:, :, :]).then_inc(kv_sb, 1)
                dve.wait_ge(km_full, l + 1)
                dve.tensor_copy(kmT[:, :, :], DB[1][:, 0, :].rearrange("p (c t) -> p c t", c=2)).then_inc(km_sb, 1)

                def z_tile(n):
                    dve.wait_ge(slots_free, l * UNITS1 + unit_done(3 + 2 * n))
                    dve.tensor_copy(z[:, :, n * UN:(n + 1) * UN], DB[n % 2][:, :, :]).then_inc(z_sb, 1)

                for n in range(4):
                    split_lo(dve, l, 4 + 2 * n)
                    z_tile(n)
                dve.wait_ge(z_sb, l * 5 + 4)

                def heads(t):
                    return z[:, t, 0:2304].rearrange("p (m h d) -> p m h d", m=2, d=HD)[:, :, 0:12, 0:16]

                def table(name, t):
                    tab = const(name).rearrange("p (t d) -> p t d", t=TT)[:, t, :]
                    return tab.unsqueeze(1).unsqueeze(1).to_broadcast([P, 2, 12, 16])

                ra = [rope_a[:, t, :].rearrange("p (m h d) -> p m h d", m=2, d=16) for t in range(TT)]
                rb = [rope_b[:, t, :].rearrange("p (m h d) -> p m h d", m=2, d=16) for t in range(TT)]
                for t in range(TT):
                    dve.tensor_tensor(ra[t], heads(t), table("cos1", t), ALU.mult).then_inc(rope_s, 1)
                for t in range(TT):
                    dve.tensor_tensor(rb[t][:, :, :, 0:8], heads(t)[:, :, :, 8:16], table("sin1", t)[:, :, :, 0:8], ALU.mult)\
                       .then_inc(rope_s, 1)
                for t in range(TT):
                    dve.tensor_tensor(rb[t][:, :, :, 8:16], heads(t)[:, :, :, 0:8], table("sin1", t)[:, :, :, 8:16], ALU.mult)\
                       .then_inc(rope_s, 1)
                dve.wait_ge(rope_s, l * 8 + 6)
                for t in range(TT):
                    dve.tensor_tensor(heads(t), ra[t], rb[t], ALU.add).then_inc(rope_s, 1)
                z_tile(4)

                def gate_inverse(g, first, n):
                    t, c0 = first // 2, COL_GATE + g * UN + first % 2 * (UN // 2)
                    v = z[:, t, c0:c0 + UN // 2] if n == 1 else z[:, :, c0:c0 + UN]
                    dve.wait_ge(g_one, l * 6 + g + 1)
                    dve.reciprocal(v, v).then_inc(g_rec, 1)

                for j in range(NJ + 1):
                    if j >= 1:
                        i, wide = j - 1, P * len(JOBS[j - 1]["blocks"])
                        dve.wait_ge(e_sb, l * NJ + j)
                        dve.reciprocal(rden[:, i:i + 1], den[:, i:i + 1]).then_inc(p_v, 1)
                        dve.wait_ge(p_v, l * (2 * NJ) + 2 * i + 1)
                        dve.tensor_scalar(S[:, i % 3, 0:wide], S[:, i % 3, 0:wide], rden[:, i:i + 1], None, ALU.mult)\
                           .then_inc(p_v, 1)
                    if j < NJ:
                        job, wide = JOBS[j], P * len(JOBS[j]["blocks"])
                        o, s_in = S[:, j % 3, 0:wide], flat[j % 2][:, 0:wide]
                        if job["kind"] == "dilated":
                            mask = const("dilated")
                            if job["t"] == 0:
                                mask = mask.rearrange("p (g b k) -> p g b k", g=3, b=2)[:, :, 1, :]
                                o = o.rearrange("p (g k) -> p g k", g=3)
                                s_in = s_in.rearrange("p (g k) -> p g k", g=3)
                        else:
                            first = {"memory": 0, "causal": P * (2 - job["t"])}[job["kind"]]
                            mask = const("causal")[:, first:first + wide]
                        dve.wait_ge(s_full, l * NJ + j + 1)
                        if j >= 3:
                            dve.wait_ge(t_full, l * NJ + j - 2)
                        dve.sem_inc(s_seen, 1)
                        dve.tensor_tensor_reduce(out=o, in0=s_in, in1=mask, scale=1.0, scalar=-3e38, op0=ALU.add,
                                                 op1=ALU.max, accum_out=mx[:, j:j + 1]).then_inc(s_v, 1)
                        dve.wait_ge(s_v, l * (2 * NJ) + 2 * j + 1)
                        dve.tensor_scalar(nmx[:, j:j + 1], mx[:, j:j + 1], -HD ** -0.5, None, ALU.mult).then_inc(s_v, 1)
                    for i in {22: (16, 17), 23: (18, 19)}.get(j, (j - 6,) if 6 <= j < 22 else ()):
                        gate_inverse(i // 4, i % 4, 1)
                dve.wait_ge(g_rec, l * 21 + 20)

                for n in range(2):
                    part = []
                    for b in range(3):
                        i, u = 3 * n + b, 24 + 2 * n + (b == 2)
                        if b == 0:
                            dve.wait_ge(pa_full, l * 2 + n + 1)
                        else:
                            dve.wait_ge(slots_free, l * UNITS1 + unit_done(u))
                        if b + n == 3:
                            dve.wait_ge(g_rec, l * 21 + 21)
                        c0 = COL_GATE + b * D + n * UN
                        part.append(z[:, :, c0:c0 + UN])
                        dve.tensor_tensor(part[b], DB[i % 2][:, :, :], part[b], ALU.mult).then_inc(pj_sb, 1)
                        y = xn[:, :, n * UN:(n + 1) * UN]
                        if b:
                            dve.wait_ge(pj_sb, l * 6 + i + 1)
                            if b == 2:
                                dve.wait_ge(y_sum, l * 4 + 2 * n + 1)
                            dve.tensor_tensor(y, part[0] if b == 1 else y, part[b], ALU.add).then_inc(y_sum, 1)
                    if n == 0:
                        gate_inverse(5, 0, 4)
                dve.wait_ge(turn_full, l * 6 + 5)
                dve.tensor_copy(hT_hi[:, 0:4, :], flat[2].rearrange("p (k t) -> p k t", k=4)).then_inc(turn_v, 1)
                for half in range(2):
                    dve.wait_ge((turn_v, turn_a)[half], l * 9 + 6)
                    k = slice(4 * half, 4 * half + 4)
                    dve.tensor_tensor(hT_lo[:, k, :], flat[2 + half].rearrange("p (k t) -> p k t", k=4), hT_hi[:, k, :].bitcast(F32),
                                      ALU.subtract).then_inc(turn_lo, 1)
                for n in range(2):
                    dve.wait_ge(slots_free, l * UNITS1 + unit_done(29 + 2 * n))
                    part = x[:, :, n * UN:(n + 1) * UN]
                    dve.tensor_tensor(part, part, DB[n][:, :, :], ALU.add).then_inc(wo_x, 1)
                dve.wait_ge(wo_x, l * 2 + 2)
                dve.wait_ge(turn_full, l * 6 + 6)
                norm(l * 2 + 2, x, xn)
                turn_gain(l * 6 + 7, g_now[:, 2, :], l * 9 + 10, l * 9 + 10)

                def low_squares(n):
                    dve.wait_ge(u_sb, l * 8 + n + 1)
                    k = slice(4 * n, 4 * n + 4)
                    dve.tensor_tensor(uT_lo[:, k, :], flat[2 + n % 2].rearrange("p (k t) -> p k t", k=4), uT_hi[:, k, :].bitcast(F32),
                                      ALU.subtract).then_inc(u_lo, 1)

                for n in range(8):
                    split_lo(dve, l, 34 + 2 * n)
                    dve.wait_ge(slots_free, l * UNITS1 + unit_done(33 + 2 * n))
                    if n >= 2:
                        dve.wait_ge(u_full, l * 8 + n - 1)
                    r = r_up[:, n % 2, :, :]
                    dve.tensor_scalar(r, DB[n % 2][:, :, :], 0.0, None, ALU.max).then_inc(relu_sb, 1)
                    dve.wait_ge(relu_sb, l * 8 + n + 1)
                    dve.tensor_tensor(r, r, DB[n % 2][:, :, :], ALU.mult).then_inc(up_sb, 1)
                    if n:
                        low_squares(n - 1)
                low_squares(7)
                for u in range(50, UNITS1, 2):
                    split_lo(dve, l, u)
                    if u in (54, 58, 62):
                        q = (54, 58, 62).index(u)
                        dve.wait_ge(mod_full, l * 3 + q + 1)
                        dve.wait_ge(bias_in, 96)
                        dve.tensor_tensor(mod_acc[:, q, :], psum[:, 4 + q, :], mod_acc[:, q, :], ALU.add).then_inc(mod_add, 1)
                for n in range(2):
                    dve.wait_ge(slots_free, l * UNITS1 + unit_done(62 + n))
                    part = x[:, :, n * UN:(n + 1) * UN]
                    dve.tensor_tensor(part, part, DB[n][:, :, :], ALU.add).then_inc(dn_x, 1)
                dve.wait_ge(dn_x, l * 2 + 2)
                dve.sem_inc(x_ready, 1)
                dve.wait_ge(turn_full, l * 6 + 8)
            vector_block2(dve, norm)

        @block.scalar
        def _(act):
            def norm(call, src, junk):
                act.activation(junk[:, 0, :], src[:, 0, :], ACT.Square, accum_out=stat[:, 0, 0:1]).then_inc(norm_a, 1)
                act.wait_ge(norm_v, call * 5 + 2)
                act.activation(stat[:, :, 2:3], stat[:, :, 1:2], ACT.Sqrt).then_inc(norm_a, 1)

            def turn_gain(call_full, gain):
                act.wait_ge(turn_full, call_full)
                for k in range(4):
                    act.activation(hT_hi[:, 4 + k, :], flat[3][:, k * T:(k + 1) * T], ACT.Copy, scale=gain[:, 4 + k:5 + k])\
                       .then_inc(turn_a, 1)

            act.wait_ge(mem_in, 16)
            norm(0, x, xn)
            act.wait_ge(zeros, 1)
            for i, name in enumerate(("c_2", "c_ctx_2")):
                act.activation(silu_c[:, :, :, i], col2[name].rearrange("p (l c) -> p l c", l=DEPTH), ACT.Silu).then_inc(silu_sb, 1)
            act.wait_ge(turn_full, 2)
            act.activation(memnT[:, 4:8, :], flat[3].rearrange("p (k t) -> p k t", k=4), ACT.Copy).then_inc(turn_a, 1)
            act.wait_ge(x_in, 16)

            with act.Fori(0, DEPTH) as l:
                def high_parts(first, last):
                    for u in range(first, last + 1):
                        split_hi(act, l, u)

                high_parts(2, 3)
                act.wait_ge(x_ready, l + 1)
                act.wait_ge(turn_full, l * 6 + 2)
                norm(l * 2 + 1, x, xn)
                act.wait_ge(gains, l + 1)
                turn_gain(l * 6 + 4, g_now[:, 0, :])
                high_parts(4, 14)
                for b in range(4):
                    nb = 4 if b < 3 else 2
                    act.wait_ge(qk_full, l * 4 + b + 1)
                    act.activation(qkT[:, 4 * b:4 * b + nb, :],
                                   flat[2 + b % 2][:, 0:nb * T].rearrange("p (k t) -> p k t", k=nb), ACT.Copy).then_inc(qk_sb, 1)
                for j in range(NJ + 1):
                    if j >= 1:
                        i, nb = j - 1, len(JOBS[j - 1]["blocks"])
                        act.wait_ge(t_full, l * NJ + j)
                        if i >= 2:
                            act.wait_ge(o_full, l * NJ + i - 1)
                        act.activation(PT[:, i % 2, 0:nb, :], flat[2][:, 0:nb * P].rearrange("p (b q) -> p b q", b=nb),
                                       ACT.Copy).then_inc(t_sb, 1)
                    if j < NJ:
                        wide = P * len(JOBS[j]["blocks"])
                        act.wait_ge(s_v, l * (2 * NJ) + 2 * j + 2)
                        act.activation(S[:, j % 3, 0:wide], S[:, j % 3, 0:wide], ACT.Exp, bias=nmx[:, j:j + 1],
                                       scale=HD ** -0.5, accum_out=den[:, j:j + 1]).then_inc(e_sb, 1)
                    if j >= 1:
                        job = JOBS[j - 1]
                        rows = slice(job["base"], job["base"] + HD)
                        act.wait_ge(o_full, l * NJ + j)
                        act.activation(oT[rows, job["out"], job["t"] * P:(job["t"] + 1) * P], flat[2][rows, 768:768 + P],
                                       ACT.Copy).then_inc(o_sb, 1)
                    if j % 2 and 15 + j // 2 < 24:
                        split_hi(act, l, 15 + j // 2)
                    if j % 4 == 3:
                        g = j // 4
                        act.wait_ge(slots_free, l * UNITS1 + unit_done(13 + 2 * g))
                        act.activation(z[:, :, COL_GATE + g * UN:COL_GATE + (g + 1) * UN], DB[3][:, :, :], ACT.Exp,
                                       scale=-1.0).then_inc(g_exp, 1)
                high_parts(28, 30)
                act.wait_ge(turn_full, l * 6 + 6)
                act.activation(hT_hi[:, 4:8, :], flat[3].rearrange("p (k t) -> p k t", k=4), ACT.Copy).then_inc(turn_a, 1)
                high_parts(31, 34)
                act.wait_ge(wo_x, l * 2 + 2)
                norm(l * 2 + 2, x, xn)
                turn_gain(l * 6 + 8, g_now[:, 2, :])
                high_parts(35, 36)
                for n in range(8):
                    high_parts(37 + 2 * n, min(38 + 2 * n, 50))
                    act.wait_ge(u_full, l * 8 + n + 1)
                    act.activation(uT_hi[:, 4 * n:4 * n + 4, :], flat[2 + n % 2].rearrange("p (k t) -> p k t", k=4),
                                   ACT.Copy).then_inc(u_sb, 1)
                high_parts(51, UNITS1 - 1)
            scalar_block2(act, norm)

        @block.gpsimd
        def _(pool):
            pool.wait_ge(cols_sb, 1)
            pool.memset(silu_c[:, :, :, :], 0.0).then_inc(zeros, 1)
            pool.memset(mod_acc, 0.0).then_inc(zeros, 1)
            pool.wait_ge(zeros, 2)
            for m in range(2):
                for q in range(3):
                    src = w["b_mod_2"][0, 4 * UN * q:4 * UN * (q + 1)].rearrange("(j n) -> j n", j=4)
                    pool.dma_start(mod_acc[m:m + 97:32, q, :], src).then_inc(bias_in, 16)
            with pool.Fori(0, DEPTH) as l:
                pool.wait_ge(turn_v, l * 9 + 1)
                pool.wait_ge(turn_a, l * 9 + 1)
                pool.tensor_copy(g_now[:, :, :], g_feat[:, :, l, :]).then_inc(gains, 1)
                pool.wait_ge(gains, l + 1)
                pool.wait_ge(silu_sb, 2)
                pool.wait_ge(mod_add, l * 3 + 1)
                pool.tensor_copy(silu_now, silu_c[:, l, :, :]).then_inc(silu_l, 1)
                for half in range(2):
                    k = slice(4 * half, 4 * half + 4)
                    gain = g_now[:, 1, k].unsqueeze(2).to_broadcast([P, 4, T])
                    pool.tensor_tensor(memT[:, k, :], memnT[:, k, :], gain, ALU.mult).then_inc(mem_g, 1)
                for u in [u for u in LO_POOL if u < 15]:
                    split_lo(pool, l, u)
                for g in range(6):
                    for u in (15 + 2 * g, 16 + 2 * g):
                        if u < 24:
                            split_lo(pool, l, u)
                    v = z[:, :, COL_GATE + g * UN:COL_GATE + (g + 1) * UN]
                    pool.wait_ge(g_exp, l * 6 + g + 1)
                    one = const("one").unsqueeze(2).to_broadcast([P, TT, UN])
                    pool.tensor_tensor(v, v, one, ALU.add).then_inc(g_one, 1)
                for u in [u for u in LO_POOL if u > 24]:
                    split_lo(pool, l, u)
            gpsimd_block2(pool)


_NAMES = ["x", "mem", "norm_mix", "w_in", "w_out", "norm_mem", "w_mem_kv", "norm_mlp", "w_up", "w_down", "norm_final",
          "c_2", "ctx_2", "c_ctx_2", "w_mod_2", "b_mod_2", "norm1_2", "w_in_2", "q_norm_2", "w_uq_2", "kv_norm_2",
          "w_ukv_2", "conv_w_2", "conv_b_2", "w_qblk_2", "w_kblk_2", "w_vblk_2", "w_gate_2", "b_gate_2", "ml_norm_2",
          "ml_skip_2", "w_out_2", "norm2_2", "w_router_2", "w_e_gate_2", "w_e_up_2", "w_e_down_2", "final_norm_2"]


def kernel(**inputs):
    import concourse.bacc as bacc
    from concourse.bass_utils import run_bass_kernel_spmd

    arrays = {name: np.ascontiguousarray(inputs[name]) for name in _NAMES}
    arrays["w_proj"] = np.concatenate([np.asarray(inputs["w_proj_" + m]) for m in "abm"], 1)
    arrays["consts"] = constants()[1]
    nc = bacc.Bacc("TRN2", target_bir_lowering=False, num_devices=1)
    views = {}
    for name, a in arrays.items():
        views[name] = nc.dram_tensor(f"in_{name}", a.shape, mybir.dt.from_np(a.dtype), kind="ExternalInput").ap()
    out = nc.dram_tensor("out_y", (1, T, D), F32, kind="ExternalOutput").ap()
    build(nc, views, out)
    result = run_bass_kernel_spmd(nc, [{f"in_{name}": a for name, a in arrays.items()}], core_ids=[0])
    return result.results[0]["out_y"]
```
